# Optimizing a Trainium2 kernel written in Bass

```python
import math
import jax, jax.numpy as jnp
from jax import lax
import numpy as np

D_MODEL = 1024
BATCH = 1
SEQ = 512
DEPTH = 2

HEAD_DIM = 64
BLOCK = 128
EPS = 1e-6
NEG = -1e30
A_HEADS = 8
A_KV_HEADS = 2
IDX_HEADS = 8
IDX_DIM = 64
TOPK_MAX = 256
LRU_WIDTH = 512
LRU_BLOCKS = 8
CONV_WIDTH = 4
LRU_C = 8.0
C_HEADS = 8
Q_LORA = 256
KV_LORA = 128
QK_NOPE = 64
QK_ROPE = 32
V_DIM = 64
ROPE_THETA = 10000.0
D_HEADS = 8
D_KV_HEADS = 2
WINDOW = 128
N_BRANCH = 4
BRANCH_WIDTH = 512
N_ALIBI = A_HEADS + D_HEADS
D_FF = 2816
IN_SPLITS = (A_HEADS * HEAD_DIM, A_KV_HEADS * HEAD_DIM, A_KV_HEADS * HEAD_DIM,
             IDX_HEADS * IDX_DIM, IDX_DIM, IDX_HEADS,
             LRU_WIDTH, LRU_WIDTH,
             Q_LORA, KV_LORA + QK_ROPE,
             D_HEADS * HEAD_DIM, D_KV_HEADS * HEAD_DIM, D_KV_HEADS * HEAD_DIM,
             N_BRANCH * D_MODEL)
IN_WIDTH = sum(IN_SPLITS)

kernel_name = "hybrid_gated_dsa_rglru_mla_swa_macaron"

def rmsnorm(x, g):
    xf = x.astype(jnp.float32)
    y = xf * lax.rsqrt(jnp.mean(xf * xf, axis=-1, keepdims=True) + EPS)
    return (y * g.astype(jnp.float32)).astype(x.dtype)

def alibi_slopes():
    i = jnp.arange(1, N_ALIBI + 1, dtype=jnp.float32)
    return 2.0 ** (-8.0 * i / N_ALIBI)

def rope(x, pos):
    half = QK_ROPE // 2
    inv = ROPE_THETA ** (-jnp.arange(half, dtype=jnp.float32) / half)
    ang = pos.astype(jnp.float32)[:, None] * inv[None, :]
    cos, sin = jnp.cos(ang)[:, None, :], jnp.sin(ang)[:, None, :]
    xf = x.astype(jnp.float32)
    x1, x2 = xf[..., :half], xf[..., half:]
    return jnp.concatenate([x1 * cos - x2 * sin, x2 * cos + x1 * sin], axis=-1).astype(x.dtype)

def to_blocks(t, nb):
    return jnp.moveaxis(t.reshape(t.shape[0], nb, BLOCK, *t.shape[2:]), 1, 0)

def from_blocks(t):
    t = jnp.moveaxis(t, 0, 1)
    return t.reshape(t.shape[0], -1, t.shape[-1])

gather_rows = jax.vmap(lambda rows, idx: rows[idx])

def swiglu(h, w_in, w_out):
    gate, up = jnp.split(h @ w_in, 2, axis=-1)
    return (jax.nn.silu(gate) * up) @ w_out

def dsa_attention(q, k, v, qi, ki, wi, slopes):
    B, S, H, Dh = q.shape
    G = k.shape[2]
    R = H // G
    nb = S // BLOCK
    topk = min(TOPK_MAX, S // 4)
    scale = Dh ** -0.5
    key_pos = jnp.arange(S)
    slopes_gr = slopes.reshape(G, R).astype(jnp.float32)
    ki32 = ki.astype(jnp.float32)

    def one_block(args):
        qb, qib, wib, start = args
        qpos = start + jnp.arange(BLOCK)
        causal = key_pos[None, :] <= qpos[:, None]
        dots = jnp.einsum('bthd,bsd->bths', qib.astype(jnp.float32), ki32)
        iscore = jnp.einsum('bth,bths->bts', wib.astype(jnp.float32), jax.nn.relu(dots))
        iscore = jnp.where(causal[None], iscore, -jnp.inf)
        _, sel = lax.top_k(iscore, topk)
        ksel = gather_rows(k, sel)
        vsel = gather_rows(v, sel)
        dist = qpos[None, :, None] - sel
        valid = dist >= 0
        s = jnp.einsum('btgrd,btkgd->btgrk', qb.reshape(B, BLOCK, G, R, Dh), ksel).astype(jnp.float32) * scale
        s = s - slopes_gr[None, None, :, :, None] * dist.astype(jnp.float32)[:, :, None, None, :]
        s = jnp.where(valid[:, :, None, None, :], s, NEG)
        p = jax.nn.softmax(s, axis=-1).astype(v.dtype)
        o = jnp.einsum('btgrk,btkgd->btgrd', p, vsel)
        return o.reshape(B, BLOCK, H * Dh)

    starts = jnp.arange(nb, dtype=jnp.int32) * BLOCK
    out = lax.map(one_block, (to_blocks(q, nb), to_blocks(qi, nb), to_blocks(wi, nb), starts))
    return from_blocks(out)

def rglru_branch(xr, xg, conv_w, conv_b, wa, ba, wx, bx, lam):
    B, S, W = xr.shape
    xc = lax.conv_general_dilated(xr, conv_w.astype(xr.dtype).reshape(CONV_WIDTH, 1, W),
                                  window_strides=(1,), padding=[(CONV_WIDTH - 1, 0)],
                                  dimension_numbers=('NWC', 'WIO', 'NWC'),
                                  feature_group_count=W) + conv_b
    xb = xc.reshape(B, S, LRU_BLOCKS, W // LRU_BLOCKS)
    r = jax.nn.sigmoid((jnp.einsum('bsni,nij->bsnj', xb, wa).reshape(B, S, W) + ba).astype(jnp.float32))
    i = jax.nn.sigmoid((jnp.einsum('bsni,nij->bsnj', xb, wx).reshape(B, S, W) + bx).astype(jnp.float32))
    log_a = -LRU_C * r * jax.nn.softplus(-lam.astype(jnp.float32))
    a = jnp.exp(log_a)
    b = jnp.sqrt(-jnp.expm1(2.0 * log_a)) * (i * xc.astype(jnp.float32))

    def combine(left, right):
        a_l, b_l = left
        a_r, b_r = right
        return a_l * a_r, a_r * b_l + b_r

    _, h = lax.associative_scan(combine, (a, b), axis=1)
    return h.astype(xr.dtype) * jax.nn.gelu(xg)

def causal_block_attention(q, k, v, scale):
    B, S, H, _ = q.shape
    nb = S // BLOCK
    key_pos = jnp.arange(S)

    def one_block(args):
        qb, start = args
        qpos = start + jnp.arange(BLOCK)
        s = jnp.einsum('bthd,bshd->bhts', qb, k).astype(jnp.float32) * scale
        s = jnp.where((key_pos[None, :] <= qpos[:, None])[None, None], s, NEG)
        p = jax.nn.softmax(s, axis=-1).astype(v.dtype)
        return jnp.einsum('bhts,bshd->bthd', p, v).reshape(B, BLOCK, -1)

    starts = jnp.arange(nb, dtype=jnp.int32) * BLOCK
    return from_blocks(lax.map(one_block, (to_blocks(q, nb), starts)))

def mla_attention(cq, ckv_full, g_q, g_kv, w_uq, w_ukv):
    B, S, _ = cq.shape
    q = (rmsnorm(cq, g_q) @ w_uq).reshape(B, S, C_HEADS, QK_NOPE + QK_ROPE)
    c_kv, k_rope = ckv_full[..., :KV_LORA], ckv_full[..., KV_LORA:]
    kv = (rmsnorm(c_kv, g_kv) @ w_ukv).reshape(B, S, C_HEADS, QK_NOPE + V_DIM)
    k_nope, v = kv[..., :QK_NOPE], kv[..., QK_NOPE:]
    pos = jnp.arange(S)
    q = jnp.concatenate([q[..., :QK_NOPE], rope(q[..., QK_NOPE:], pos)], axis=-1)
    k_rope = jnp.broadcast_to(rope(k_rope[:, :, None, :], pos), (B, S, C_HEADS, QK_ROPE))
    k = jnp.concatenate([k_nope, k_rope], axis=-1)
    return causal_block_attention(q, k, v, (QK_NOPE + QK_ROPE) ** -0.5)

def sliding_window_attention(q, k, v, sinks, slopes):
    B, S, H, Dh = q.shape
    G = k.shape[2]
    R = H // G
    nb = S // BLOCK
    qb = q.reshape(B, nb, BLOCK, G, R, Dh)
    kb = k.reshape(B, nb, BLOCK, G, Dh)
    vb = v.reshape(B, nb, BLOCK, G, Dh)
    prev = lambda t: jnp.concatenate([jnp.zeros_like(t[:, :1]), t[:, :-1]], axis=1)
    kw = jnp.concatenate([prev(kb), kb], axis=2)
    vw = jnp.concatenate([prev(vb), vb], axis=2)
    blk = jnp.arange(nb)[:, None] * BLOCK
    qpos = blk + jnp.arange(BLOCK)[None, :]
    kpos = blk - BLOCK + jnp.arange(2 * BLOCK)[None, :]
    dist = qpos[:, :, None] - kpos[:, None, :]
    valid = (kpos[:, None, :] >= 0) & (dist >= 0) & (dist < WINDOW)
    s = jnp.einsum('bntgrd,bnkgd->bngrtk', qb, kw).astype(jnp.float32) * (Dh ** -0.5)
    s = s - slopes.reshape(G, R).astype(jnp.float32)[None, None, :, :, None, None] * dist.astype(jnp.float32)[None, :, None, None, :, :]
    s = jnp.where(valid[None, :, None, None], s, NEG)
    sink = jnp.broadcast_to(sinks.reshape(G, R).astype(jnp.float32)[None, None, :, :, None, None], s.shape[:-1] + (1,))
    p = jax.nn.softmax(jnp.concatenate([s, sink], axis=-1), axis=-1)[..., :-1].astype(v.dtype)
    o = jnp.einsum('bngrtk,bnkgd->bntgrd', p, vw)
    return o.reshape(B, S, H * Dh)

def token_mixer(h, w_in, conv_w, conv_b, lru_wa, lru_ba, lru_wx, lru_bx, lru_lambda,
                mla_g_q, mla_g_kv, mla_w_uq, mla_w_ukv, swa_sinks, w_branch, w_out):
    B, S, _ = h.shape
    z = h @ w_in
    splits = np.cumsum(IN_SPLITS)[:-1].tolist()
    (a_q, a_k, a_v, i_q, i_k, i_w, r_x, r_g, c_q, c_kv, d_q, d_k, d_v, gates) = jnp.split(z, splits, axis=-1)
    slopes = alibi_slopes()
    slopes_d, slopes_a = slopes[:D_HEADS], slopes[D_HEADS:]
    y_a = dsa_attention(a_q.reshape(B, S, A_HEADS, HEAD_DIM), a_k.reshape(B, S, A_KV_HEADS, HEAD_DIM),
                        a_v.reshape(B, S, A_KV_HEADS, HEAD_DIM), i_q.reshape(B, S, IDX_HEADS, IDX_DIM),
                        i_k, i_w, slopes_a)
    y_b = rglru_branch(r_x, r_g, conv_w, conv_b, lru_wa, lru_ba, lru_wx, lru_bx, lru_lambda)
    y_c = mla_attention(c_q, c_kv, mla_g_q, mla_g_kv, mla_w_uq, mla_w_ukv)
    y_d = sliding_window_attention(d_q.reshape(B, S, D_HEADS, HEAD_DIM), d_k.reshape(B, S, D_KV_HEADS, HEAD_DIM),
                                   d_v.reshape(B, S, D_KV_HEADS, HEAD_DIM), swa_sinks, slopes_d)
    ys = jnp.stack([y_a, y_b, y_c, y_d], axis=2)
    proj = jnp.einsum('bsnw,nwd->bsnd', ys, w_branch)
    g = jax.nn.sigmoid(gates.reshape(B, S, N_BRANCH, D_MODEL))
    return jnp.sum(g * proj, axis=2) @ w_out

def sandwich(x, y_fn, g_pre, g_post, shift, scale, gate, resid_w):
    h = rmsnorm(x, g_pre) * (1.0 + scale) + shift
    return x + resid_w * gate * rmsnorm(y_fn(h), g_post)

def setup_inputs(seed: int = 0) -> dict:
    key = jax.random.key(seed)
    ks = jax.random.split(key, 24)
    f32 = jnp.float32
    nrm = lambda k, shape, fan_in: jax.random.normal(k, shape, f32) * (fan_in ** -0.5)
    bw = LRU_WIDTH // LRU_BLOCKS
    u = jax.random.uniform(ks[14], (DEPTH, LRU_WIDTH), f32, 0.9, 0.999)
    s = u ** (1.0 / LRU_C)
    lru_lambda = jnp.log(s) - jnp.log1p(-s)
    return {
        "x": jax.random.normal(ks[0], (BATCH, SEQ, D_MODEL), f32),
        "c": jax.random.normal(ks[1], (BATCH, D_MODEL), f32),
        "w_ada": 0.5 * nrm(ks[2], (DEPTH, D_MODEL, 9 * D_MODEL), D_MODEL),
        "b_ada": 0.02 * jax.random.normal(ks[3], (DEPTH, 9 * D_MODEL), f32),
        "norm_g": 1.0 + 0.05 * jax.random.normal(ks[4], (DEPTH, 6, D_MODEL), f32),
        "ffn1_w_in": nrm(ks[5], (DEPTH, D_MODEL, 2 * D_FF), D_MODEL),
        "ffn1_w_out": nrm(ks[6], (DEPTH, D_FF, D_MODEL), D_FF),
        "w_in": nrm(ks[7], (DEPTH, D_MODEL, IN_WIDTH), D_MODEL),
        "conv_w": nrm(ks[8], (DEPTH, CONV_WIDTH, LRU_WIDTH), CONV_WIDTH),
        "conv_b": 0.02 * jax.random.normal(ks[9], (DEPTH, LRU_WIDTH), f32),
        "lru_wa": nrm(ks[10], (DEPTH, LRU_BLOCKS, bw, bw), bw),
        "lru_ba": 0.02 * jax.random.normal(ks[11], (DEPTH, LRU_WIDTH), f32),
        "lru_wx": nrm(ks[12], (DEPTH, LRU_BLOCKS, bw, bw), bw),
        "lru_bx": 0.02 * jax.random.normal(ks[13], (DEPTH, LRU_WIDTH), f32),
        "lru_lambda": lru_lambda,
        "mla_g_q": 1.0 + 0.05 * jax.random.normal(ks[15], (DEPTH, Q_LORA), f32),
        "mla_g_kv": 1.0 + 0.05 * jax.random.normal(ks[16], (DEPTH, KV_LORA), f32),
        "mla_w_uq": nrm(ks[17], (DEPTH, Q_LORA, C_HEADS * (QK_NOPE + QK_ROPE)), Q_LORA),
        "mla_w_ukv": nrm(ks[18], (DEPTH, KV_LORA, C_HEADS * (QK_NOPE + V_DIM)), KV_LORA),
        "swa_sinks": 0.5 * jax.random.normal(ks[19], (DEPTH, D_HEADS), f32),
        "w_branch": nrm(ks[20], (DEPTH, N_BRANCH, BRANCH_WIDTH, D_MODEL), BRANCH_WIDTH),
        "w_out": nrm(ks[21], (DEPTH, D_MODEL, D_MODEL), D_MODEL),
        "ffn2_w_in": nrm(ks[22], (DEPTH, D_MODEL, 2 * D_FF), D_MODEL),
        "ffn2_w_out": nrm(ks[23], (DEPTH, D_FF, D_MODEL), D_FF),
    }

def reference(x, c, w_ada, b_ada, norm_g, ffn1_w_in, ffn1_w_out, w_in, conv_w, conv_b,
              lru_wa, lru_ba, lru_wx, lru_bx, lru_lambda, mla_g_q, mla_g_kv, mla_w_uq, mla_w_ukv,
              swa_sinks, w_branch, w_out, ffn2_w_in, ffn2_w_out):
    B = x.shape[0]
    for l in range(DEPTH):
        mod = (jax.nn.silu(c) @ w_ada[l] + b_ada[l]).reshape(B, 9, 1, D_MODEL)
        g = norm_g[l]
        x = sandwich(x, lambda h: swiglu(h, ffn1_w_in[l], ffn1_w_out[l]),
                     g[0], g[1], mod[:, 0], mod[:, 1], mod[:, 2], 0.5)
        x = sandwich(x, lambda h: token_mixer(h, w_in[l], conv_w[l], conv_b[l], lru_wa[l], lru_ba[l],
                                              lru_wx[l], lru_bx[l], lru_lambda[l], mla_g_q[l], mla_g_kv[l],
                                              mla_w_uq[l], mla_w_ukv[l], swa_sinks[l], w_branch[l], w_out[l]),
                     g[2], g[3], mod[:, 3], mod[:, 4], mod[:, 5], 1.0)
        x = sandwich(x, lambda h: swiglu(h, ffn2_w_in[l], ffn2_w_out[l]),
                     g[4], g[5], mod[:, 6], mod[:, 7], mod[:, 8], 0.5)
    return x


_drawn_inputs = setup_inputs


def setup_inputs(seed=0):
    import zlib

    import numpy as np

    out = dict(_drawn_inputs(seed))
    spreads = {}
    factors = {'lru_ba': 200.0,
     'lru_bx': 64.0,
     'mla_g_q': 8.0,
     'mla_g_kv': 8.0,
     'swa_sinks': 52.633,
     'conv_b': 8.0,
     'lru_wa': 3.874}
    for name, (base, spread) in spreads.items():
        noise = np.random.default_rng([zlib.crc32(name.encode()), seed]).standard_normal(out[name].shape)
        drawn = base * np.exp(spread * noise) if base else spread * noise
        out[name] = __import__('jax').numpy.asarray(drawn.astype(out[name].dtype))
    for name, factor in factors.items():
        out[name] = (out[name] * factor).astype(out[name].dtype)
    return out
```

```python
from contextlib import ExitStack

import numpy as np

import concourse.bass as bass
from concourse import mybir

F32 = mybir.dt.float32
F32R = mybir.dt.float32r
ALU = mybir.AluOpType
ACT = mybir.ActivationFunctionType
AX_X = mybir.AxisListType.X

P = 128
DEPTH, D, T, FF = 2, 1024, 512, 2816
KD = D // P
TB = T // P
FT = FF // P
HEADS, HD = 8, 64
NOPE, ROPE = 64, 32
TOPK = min(256, T // 4)
NADA = 9
EPS = 1e-6
BIG = 1e30
A_SCALE = HD ** -0.5
C_SCALE = (NOPE + ROPE) ** -0.5
SLOPES = [2.0 ** (-8.0 * i / 16) for i in range(1, 17)]
SLOPE = {"D": SLOPES[:8], "A": SLOPES[8:]}
LRU_T = 512 // P
UNROLL = 4
RING, LEAD = 4, 3

_PAR = [("b_ada", NADA * KD), ("norm_g", 6 * KD), ("conv_w", 4 * LRU_T), ("conv_b", LRU_T), ("ba", LRU_T),
        ("bx", LRU_T), ("lam", LRU_T), ("g_q", 2), ("g_kv", 1), ("sink", HEADS)]
PAR, _at = {}, 0
for _n, _w in _PAR:
    PAR[_n] = _at
    _at += _w
NPAR = _at
ADA_ORDER = [2, 3, 4, 5, 6, 7, 8, 0, 1]
SLOT_OF = {c: i for i, c in enumerate(ADA_ORDER)}



def mixer_schedule():
    def att(br, fill, every):
        fill = list(fill)
        for s in range(HEADS * TB + 4):
            yield ("att", br, s)
            if br == "C":
                for r in (3 * s, 3 * s + 1, 3 * s + 2):
                    if r < 16 * (TB - 1):
                        yield ("topk", r // 16 + 1, r % 16)
            if fill and s % every == every - 1:
                yield fill.pop(0)
        yield from fill

    def merge(n):
        for mp in range(KD // 2):
            yield ("gate", n, 2 * mp)
            yield ("gate", n, 2 * mp + 1)
            yield ("branch", n, mp)

    yield from [("in", "cq", 0), ("in", "cq", 1), ("in", "ckv", 0), ("cstats",), ("in", "misc", 0), ("cbcast",),
                ("in", "iq", 0), ("cnorm",), ("in", "iq", 1), ("in", "iq", 2), ("in", "iq", 3), ("in", "ik", 0),
                ("uq", 0), ("uq", 1), ("ukv",), ("wi",)]
    for b in range(1, TB):
        for h in range(HEADS):
            yield ("index", b, h)
    yield from att("C", [("in", "aq", j) for j in range(4)] + [("in", "ak", 0), ("in", "av", 0)], 5)
    yield ("vtok", "A")
    yield from att("A", merge("C"), 2)
    yield from [("in", "dq", j) for j in range(4)] + [("in", "dk", 0), ("in", "dv", 0), ("vtok", "D")]
    yield from att("D", merge("A"), 2)
    yield from [("in", "rx", j) for j in range(LRU_T)] + [("in", "rg", j) for j in range(LRU_T)]
    fill = list(merge("D"))
    for j in range(LRU_T):
        yield ("conv", j)
        yield fill.pop(0)
        yield ("lru", j)
        yield fill.pop(0)
    yield ("sqrt",)
    for j in range(LRU_T):
        yield ("scan", j)
        yield fill.pop(0)
    yield from fill
    yield from merge("B")
    yield ("split_merged",)
    for m in range(KD):
        yield ("out", m)


MIXER = list(mixer_schedule())
BRANCHES = ["C", "A", "D", "B"]
Y_OF = {n: i % 2 for i, n in enumerate(BRANCHES)}
ATT = ["C", "A", "D"]
STEPS = HEADS * TB
UNIT_KINDS = ("in", "uq", "ukv", "gate", "branch", "out")
MIX_UNITS = [it for it in MIXER if it[0] in UNIT_KINDS]
U_BANK = {it: c for c, it in enumerate(it for it in MIXER if it[0] in ("in", "gate"))}
V_BANK, _d = {}, 0
for _it in MIXER:
    if _it[0] == "att" and _it[2] >= 11 and (_it[2] - 11) % HEADS == 0 and (_it[2] - 11) // HEADS < TB:
        V_BANK[("y", _it[1], (_it[2] - 11) // HEADS)] = _d
        _d += 1
    if _it[0] == "branch":
        V_BANK[("proj", _it[1], 2 * _it[2])] = _d
        V_BANK[("proj", _it[1], 2 * _it[2] + 1)] = _d + 1
        _d += 2
V_USES = _d

FFN_UNITS = 2 * FT + FT
U_FFN = (0, FFN_UNITS + len(MIX_UNITS))
U_MIX = FFN_UNITS
UNITS = 2 * FFN_UNITS + len(MIX_UNITS)
assert UNITS % RING == 0
U_OF = {it: U_MIX + i for i, it in enumerate(MIX_UNITS)}
ADA_FFN = (7, 2)


class Signal:

    def __init__(self, sem, per_layer, start=0):
        self.sem, self.per_layer, self.start = sem, per_layer, start

    def at(self, l, n):
        return l * self.per_layer + (self.start + n)


def trunk_kernel(nc, stream, ada, ada0, pars, par0, cvec, consts, mixc, lruw, x_in, out):
    with ExitStack() as ctx:
        base = 16512
        marks = {}

        def at(name, shape, dt, where):
            return nc.alloc_sbuf_tensor_at(name, shape, dt, offset=base + where)

        K = 1024
        x = at("x", [P, KD, T], F32, 0)
        hH = at("h_high", [P, KD, T], F32R, 16 * K)
        hL = at("h_low", [P, KD, T], F32R, 32 * K)
        raw = at("w_raw", [P, RING, 1024], F32, 48 * K)
        wH = at("w_high", [P, RING, 1024], F32R, 64 * K)
        wL = at("w_low", [P, RING, 1024], F32R, 80 * K)
        M0 = 96 * K
        fH = at("ffn_high", [P, FT, T], F32R, M0)
        fL = at("ffn_low", [P, FT, T], F32R, M0 + FT * 2 * K)
        Z0 = M0 + 88 * K
        tanh_g = at("tanh_gate", [P, 2, T], F32, Z0)
        act = at("ffn_act", [P, 2, T], F32, Z0 + 4 * K)
        X0 = Z0 + 8 * K
        ada_raw = at("ada_raw", [P, 2, 1024], F32, X0)
        ada_acc = at("ada_acc", [P, 1024], F32, X0 + 8 * K)
        sq = at("squares", [P, 2, T], F32, Z0)
        rstd = at("rstd", [P, T], F32, Z0 + 4 * K)
        diag = at("diag", [P, TB, P], F32, Z0 + 6 * K)
        diag2 = at("diag2", [P, 2, TB, P], F32, Z0 + 4 * K)
        y_half = at("y_half", [P, KD // 2, T], F32, X0)
        tu = at("norm_tmp", [P, 2, T], F32, X0 + 8 * K)
        yH = [at(f"y_high{i}", [P, 4, T], F32R, M0 + 16 * K * i) for i in range(2)]
        yL = [at(f"y_low{i}", [P, 4, T], F32R, M0 + 16 * K * i + 8 * K) for i in range(2)]
        qC = at("q_mla", [P, HEADS, T], F32, M0 + 16 * K)
        kC = at("k_mla", [P, HEADS, T], F32, M0 + 32 * K)
        vC = at("v_mla", [P, TB, T], F32, X0)
        latent = at("latent", [P, 3, T], F32, M0 + 32 * K)
        merged = at("merged", [P, KD, T], F32, M0 + 32 * K)
        mixcs = at("mixer_consts", [P, 4 * T + 2 * P], F32, M0 + 48 * K)
        dist, causal, rope_q, rope_k = (mixcs[:, i * T:(i + 1) * T] for i in range(4))
        window = mixcs[:, 4 * T:4 * T + 2 * P]
        S0 = M0 + 57 * K
        s_sb = at("scores_sb", [P, 2, T], F32, S0)
        pt_sb = at("probs_t", [P, 2, T], F32, S0 + 4 * K)
        relu_sb = at("relu_dots", [P, 2, T], F32, S0 + 4 * K)
        bias_sb = at("bias_sb", [P, T], F32, S0 + 8 * K)
        y_tok = at("y_tok", [P, T], F32, S0 + 10 * K)
        V0 = M0 + 69 * K
        iq = at("iq", [P, 4, T], F32, V0)
        ik = at("ik", [P, T], F32, V0 + 8 * K)
        pick = {b: at(f"pick{b}", [P, P * (b + 1)], F32, V0 + 10 * K + 4 * P * [0, 0, 2, 5][b]) for b in range(1, TB)}
        misc = at("misc", [P, T], F32, V0 + 15 * K)
        krope = at("krope", [P, T], F32, V0 + 17 * K)
        aq = at("aq", [P, 4, T], F32, V0)
        ak = at("ak", [P, T], F32, V0 + 8 * K)
        v_tok = {"A": at("v_tok_a", [P, TB, P], F32, V0 + 15 * K), "D": at("v_tok_d", [P, TB, P], F32, V0 + 17 * K)}
        av = at("av", [P, T], F32, V0 + 17 * K)
        dq = at("dq", [P, 4, T], F32, X0)
        dk = at("dk", [P, T], F32, M0 + 54 * K)
        dv = at("dv", [P, T], F32, M0 + 52 * K)
        gate_t = at("gate_tanh", [P, 2, T], F32, Z0)
        gated = at("gated", [P, 2, T], F32, Z0 + 4 * K)
        PAD = 3
        rx = at("rx", [P, LRU_T, PAD + T], F32, V0)
        ix = at("gated_x", [P, LRU_T, PAD + T], F32, V0)
        rg = at("rg", [P, LRU_T, T], F32, V0 + 8 * K + 64)
        lru_w = at("lru_w", [P, 2 * LRU_T, P], F32, M0 + 48 * K)
        lru_a = at("lru_a", [P, LRU_T, T], F32, X0)
        lru_v = at("lru_v", [P, LRU_T, T], F32, S0)
        xc = at("xc", [P, T], F32, S0 + 8 * K)
        ti = at("ti", [P, T], F32, S0 + 10 * K)
        tr = at("tr", [P, T], F32, M0 + 52 * K)
        a_sq = at("a_sq", [P, T], F32, M0 + 54 * K)
        C0 = X0 + 12 * K
        small = {}

        def tiny(name, n):
            small[name] = at(name, [P, n], F32, C0 + marks.setdefault("at", 0))
            marks["at"] += (4 * n + 31) // 32 * 32
            return small[name]

        ident = tiny("ident", P)
        ones = tiny("ones", P)
        parv = tiny("parv", NPAR)
        all_par = at("all_par", [P, DEPTH, NPAR], F32, C0 + marks["at"])
        marks["at"] += (4 * DEPTH * NPAR + 31) // 32 * 32
        mod = tiny("mod", NADA * KD)
        vecA = tiny("vec_scale", KD)
        vecC = tiny("vec_gate", KD)
        cs = tiny("silu_c", KD)
        ms = tiny("mean_sq", 8)
        rs = tiny("rstd_tok", 8)
        mhalf = tiny("minus_half", 8)
        wi = tiny("wi", TB * 8)
        top8 = tiny("top8", 8)
        nmax = tiny("neg_max", 16)
        rsum = tiny("row_sum", 16)
        recip = tiny("recip", 8)
        ctmp = top8
        skt = tiny("sink_tmp", 16)
        nsink = parv[:, PAR["sink"]:PAR["sink"] + HEADS]
        lruv4 = tiny("lru_vectors", 4 * LRU_T)
        hba, hbx, sp4, nsp4 = (lruv4[:, LRU_T * i:LRU_T * (i + 1)] for i in range(4))
        lt = [skt[:, LRU_T * i:LRU_T * (i + 1)] for i in range(4)]
        assert base + C0 + marks["at"] <= nc.sbuf_usable_end, base + C0 + marks["at"] - nc.sbuf_usable_end

        bank = [ctx.enter_context(nc.psum_tensor(f"bank{i}", [P, T], F32)) for i in range(8)]

        def sig(name, per_layer, start=0):
            return Signal(ctx.enter_context(nc.semaphore(name)), per_layer, start)

        per_slot = UNITS // RING
        raw_full = [sig(f"raw_full{i}", 16 * per_slot) for i in range(RING)]
        hi_ready = [sig(f"hi_ready{i}", per_slot) for i in range(RING)]
        lo_ready = [sig(f"lo_ready{i}", per_slot, 1) for i in range(RING)]
        unit_done = [sig(f"unit_done{i}", per_slot, 1) for i in range(RING)]
        consts_in = sig("consts_in", 0)
        ada_full = [sig(f"ada_full{i}", 16 * NADA * 4, 16 * 8) for i in range(2)]
        ada_used = sig("ada_used", 8 * NADA, 16 + 2)
        ada_free = sig("ada_free", 2, 1)
        ada_sum = sig("ada_sum", NADA, 2 + 1)
        mod_ready = sig("mod_ready", NADA, 2)
        c_tanh = sig("c_tanh", 0)
        silu_ready = sig("silu_ready", 0)
        setup_done = sig("setup_done", 0)
        pair_done = sig("pair_done", 2 * FT, 2)
        gate_tanh = sig("ffn_gate_tanh", 2 * FT)
        ffn_hi = sig("ffn_hi", 2 * FT)
        ffn_lo = sig("ffn_lo", 2 * FT, 2)
        NB = 3
        CN = 3
        sq_ready = sig("sq_ready", 2 * KD * NB + CN, KD)
        sq_used = sig("sq_used", 2 * KD * NB + CN, KD)
        y_saved = sig("y_saved", NB * 4)
        ms_ready = sig("ms_ready", 2 * NB + 1, 1)
        rs_ready = sig("rs_ready", 2 * NB + 1, 1)
        diag_ready = sig("diag_ready", 2 * NB + 1, 1)
        bc_ready = sig("bcast_ready", 2 * NB + 1, 1)
        rstd_ready = sig("rstd_ready", NB)
        x_ready = sig("x_ready", KD * NB)
        u_ready = sig("u_ready", KD * NB + CN, KD)
        hh_ready = sig("h_high_ready", KD * NB + CN, KD)
        h_ready = sig("h_ready", KD * NB + CN, KD)
        mixc_in = sig("mixer_consts_in", 16)
        lru_in = sig("lru_w_in", 16)
        u_evicted = sig("u_evicted", len(U_BANK), 2)
        v_evicted = sig("v_evicted", V_USES, 2)
        qn_evicted = sig("q_nope_evicted", HEADS)
        qr_evicted = sig("q_rope_evicted", HEADS)
        kv_done = sig("kv_done", 11)
        kv_evicted = sig("kv_evicted", 12)
        kr_ready = sig("k_rope_ready", 1)
        wi_psum = sig("wi_psum", 1)
        wi_ready = sig("wi_ready", 1)
        NI = HEADS * (TB - 1)
        dots_ready = sig("dots_ready", NI)
        relu_ready = sig("relu_ready", NI)
        index_added = sig("index_added", NI)
        NS = STEPS * len(ATT)
        scores_ready = sig("scores_ready", NS)
        scores_seen = sig("scores_seen", STEPS)
        shifted = sig("shifted", NS)
        probs_ready = sig("probs_ready", NS)
        pt_ready = sig("pt_ready", NS)
        pt_evicted = sig("pt_evicted", NS)
        pv_done = sig("pv_done", NS)
        sink_sum = sig("sink_sum", TB)
        sink_exp = sig("sink_exp", TB)
        ytok_ready = sig("y_tok_ready", TB * len(ATT))
        ytr_ready = sig("y_t_ready", TB * len(ATT))
        yhi_ready = sig("y_high_ready", TB * len(ATT) + LRU_T)
        vt_psum = sig("v_t_psum", 2)
        vt_ready = sig("v_t_ready", 2)
        yb_ready = sig("yb_ready", LRU_T)
        yb_lo = sig("yb_lo", LRU_T)
        conv_ready = sig("conv_ready", LRU_T)
        lru_psum = sig("lru_psum", LRU_T)
        ti_ready = sig("ti_ready", LRU_T)
        asq_ready = sig("a_sq_ready", LRU_T)
        lruv_ready = sig("lru_v_ready", LRU_T)
        rg_sq = sig("rg_sq", LRU_T)
        gelu_in = sig("gelu_in", LRU_T)
        gelu_t = sig("gelu_tanh", LRU_T)
        sqrt_ready = sig("sqrt_ready", 1)
        merged_ready = sig("merged_ready", KD)
        mhi_ready = sig("merged_high", KD)
        mlo_ready = sig("merged_low", KD)
        pads_ready = sig("pads_ready", 1)
        sp_exp = sig("softplus_exp", 1)
        sp_in = sig("softplus_in", 1)
        lru_params = sig("lru_params", 1)
        stored = sig("stored", 0)

        def use_of(l, u):
            if u >= UNITS:
                l, u = l + 1, u - UNITS
            return l, u % RING, u // RING

        def split_high(eng, l, u, i=0):
            l, slot, n = use_of(l, u)
            eng.wait_ge(raw_full[slot].sem, raw_full[slot].at(l, 16 * (n + i + 1)))
            eng.wait_ge(unit_done[slot].sem, unit_done[slot].at(l, n + i))
            eng.activation(wH[:, slot], raw[:, slot], ACT.Copy).then_inc(hi_ready[slot].sem, 1)

        def split_low(eng, l, u, i=0):
            l, slot, n = use_of(l, u)
            eng.wait_ge(hi_ready[slot].sem, hi_ready[slot].at(l, n + i + 1))
            eng.tensor_tensor(wL[:, slot], raw[:, slot], wH[:, slot].bitcast(F32), ALU.subtract
                              ).then_inc(lo_ready[slot].sem, 1)

        def unit_ready(eng, l, u, i=0):
            l, slot, n = use_of(l, u)
            eng.wait_ge(lo_ready[slot].sem, lo_ready[slot].at(l, n + i + 1))
            return slot

        def wait_unit(eng, l, u, i=0):
            l, slot, n = use_of(l, u)
            eng.wait_ge(unit_done[slot].sem, unit_done[slot].at(l, n + i + 1))

        def product(eng, o, slot, col, rows, rhs_h, rhs_l, first, last):
            a, b = wH[rows, slot, col:col + P], wL[rows, slot, col:col + P]
            eng.matmul(o, a, rhs_h, start=first, stop=False)
            eng.matmul(o, a, rhs_l, start=False, stop=False)
            return eng.matmul(o, b, rhs_h, start=False, stop=last)

        def sq_at(n, part):
            return 2 * KD * n + KD * part + (CN if n > 0 else 0)

        def norm_at(n, part):
            return 2 * n + part + (1 if n > 0 else 0)

        def h_at(n):
            return KD * n + (CN if n > 0 else 0)

        block = ctx.enter_context(nc.Block())

        @block.sync
        def _(sp):
            sp.dma_start(parv[:, 0:3 * KD], par0).then_inc(consts_in.sem, 16)
            sp.dma_start(ident[:, :], consts[:, 0:P]).then_inc(consts_in.sem, 16)
            sp.dma_start(ones[:, :], consts[:, P:2 * P]).then_inc(consts_in.sem, 16)
            sp.dma_start(ctmp[:, :], cvec).then_inc(consts_in.sem, 16)
            sp.dma_start(all_par[:, :, :], pars).then_inc(consts_in.sem, 16)
            for j in range(KD):
                sp.dma_start(x[:, j, :], x_in[:, j, :]).then_inc(consts_in.sem, 16)

            def load_unit(l, u, i=0):
                ll, slot, n = use_of(l, u)
                sp.wait_ge(lo_ready[slot].sem, lo_ready[slot].at(ll, n + i))
                src = stream[bass.ds(l * UNITS + u + RING * i, 1)]
                sp.dma_start(raw[:, slot], src.rearrange("a p n -> p (a n)")).then_inc(raw_full[slot].sem, 16)

            def load_ada(s, src, l, n):
                sp.wait_ge(ada_used.sem, ada_used.at(l, n + s - 1))
                sp.dma_start(ada_raw[:, s % 2], src.rearrange("a b p n -> p (a b n)")).then_inc(
                    ada_full[s % 2].sem, 16)

            for s in range(16):
                if s >= 2:
                    sp.wait_ge(ada_used.sem, 2 + s - 1)
                sp.dma_start(ada_raw[:, s % 2], ada0[s]).then_inc(ada_full[s % 2].sem, 16)
            for u in range(RING):
                sp.dma_start(raw[:, u], stream[u]).then_inc(raw_full[u].sem, 16)

            with sp.Fori(0, DEPTH) as l:
                for f in range(2):
                    def turn(i, ada_on):
                        for j in range(4):
                            if ada_on:
                                if j == 0:
                                    sp.wait_ge(ada_free.sem, ada_free.at(l, f))
                                for s in (2 * j, 2 * j + 1):
                                    c = i + 7 * f
                                    load_ada(s, ada[bass.ds(l * NADA + c, 1), s:s + 1], l, 8 * c)
                            load_unit(l, U_FFN[f] + j + RING, i)
                    with sp.Fori(0, ADA_FFN[f]) as i:
                        turn(i, True)
                    with sp.Fori(ADA_FFN[f], FT // 2) as i:
                        turn(i, False)
                    for v in range(FT):
                        load_unit(l, U_FFN[f] + 2 * FT + v + RING)
                    if f == 0:
                        sp.wait_ge(x_ready.sem, x_ready.at(l, KD))
                        sp.dma_start(mixcs[:, :], mixc).then_inc(mixc_in.sem, 16)
                        for it in MIX_UNITS:
                            load_unit(l, U_OF[it] + RING)
                            if it == ("in", "rx", LRU_T - 1):
                                sp.wait_ge(pv_done.sem, pv_done.at(l, NS))
                                sp.dma_start(lru_w[:, :, :], lruw[bass.ds(l, 1)].rearrange("a p t n -> p (a t) n")
                                             ).then_inc(lru_in.sem, 16)
            for j in range(KD):
                sp.wait_ge(x_ready.sem, x_ready.at(DEPTH - 1, 2 * KD + j + 1))
                sp.dma_start(out[:, j, :], x[:, j, :]).then_inc(stored.sem, 16)
            sp.wait_ge(stored.sem, 16 * KD)
            for slot in range(RING):
                sp.wait_ge(raw_full[slot].sem, raw_full[slot].at(DEPTH, 16))

        @block.gpsimd
        def _(pool):
            pool.memset(mhalf[:, :], -0.5).then_inc(setup_done.sem, 1)
            pool.wait_ge(setup_done.sem, 1)

            def rsqrt(l, n, width):
                pool.wait_ge(ms_ready.sem, ms_ready.at(l, n + 1))
                pool.tensor_tensor(rs[:, 0:width], ms[:, 0:width], mhalf[:, 0:width], ALU.pow
                                   ).then_inc(rs_ready.sem, 1)

            rsqrt(0, -1, TB)
            with pool.Fori(0, DEPTH) as l:
                for f in range(2):
                    def turn(i):
                        for pp in range(2):
                            pool.wait_ge(ffn_hi.sem, ffn_hi.at(l, f * FT + 2 * i + pp + 1))
                            m = bass.ds(2 * i + pp, 1)
                            pool.tensor_tensor(fL[:, m, :], act[:, pp:pp + 1, :], fH[:, m, :].bitcast(F32),
                                               ALU.subtract).then_inc(ffn_lo.sem, 1)
                    with pool.Fori(0, FT // 2) as i:
                        turn(i)
                    if f == 0:
                        rsqrt(l, norm_at(0, 0), TB)
                        rsqrt(l, norm_at(0, 1), TB)
                        rsqrt(l, 2, 2 * TB)
                        rsqrt(l, norm_at(1, 0), TB)
                        rsqrt(l, norm_at(1, 1), TB)
                    else:
                        rsqrt(l, norm_at(2, 0), TB)
                        rsqrt(l, norm_at(2, 1), TB)

        def evict(s, l, it, dst, scale=1.0):
            wait_unit(s, l, U_OF[it])
            s.activation(dst, bank[U_BANK[it] % 2][:, :], ACT.Copy, scale=scale).then_inc(u_evicted.sem, 1)

        def att_index(br, st):
            return STEPS * ATT.index(br) + st

        def keys(br, st):
            b, h = st // HEADS, st % HEADS
            k0 = max(0, b - 1) if br == "D" else 0
            return b, h, k0, b + 1 - k0

        def scalar_mixer(s, l, split_high, square, high_parts):
            for it in MIXER:
                kind = it[0]
                if kind in UNIT_KINDS:
                    split_high(s, l, U_OF[it] + LEAD)
                if kind == "in":
                    name, j = it[1], it[2]
                    if name == "cq":
                        evict(s, l, it, latent[:, j])
                    elif name == "ckv":
                        evict(s, l, it, latent[:, 2])
                    elif name == "misc":
                        evict(s, l, it, misc[:, :])
                    elif name == "iq":
                        evict(s, l, it, iq[:, j])
                    elif name == "ik":
                        evict(s, l, it, ik[:, :])
                    elif name == "aq":
                        if j == 0:
                            s.wait_ge(relu_ready.sem, relu_ready.at(l, NI))
                        evict(s, l, it, aq[:, j], -A_SCALE)
                    elif name == "ak":
                        evict(s, l, it, ak[:, :])
                    elif name == "av":
                        evict(s, l, it, av[:, :])
                    elif name == "dq":
                        if j == 0:
                            s.wait_ge(pv_done.sem, pv_done.at(l, STEPS))
                        evict(s, l, it, dq[:, j], -A_SCALE)
                    elif name == "dk":
                        evict(s, l, it, dk[:, :])
                    elif name == "dv":
                        evict(s, l, it, dv[:, :])
                    elif name == "rx":
                        if j == 0:
                            s.wait_ge(pads_ready.sem, pads_ready.at(l, 1))
                            s.wait_ge(pv_done.sem, pv_done.at(l, 2 * STEPS))
                        evict(s, l, it, rx[:, j, PAD:PAD + T])
                    elif name == "rg":
                        evict(s, l, it, rg[:, j])
                elif kind == "gate":
                    n, m = it[1], it[2]
                    use = V_BANK.get(("proj", n, m - 2)) if m >= 2 else None
                    if use is None and n != "C":
                        use = V_BANK[("proj", BRANCHES[BRANCHES.index(n) - 1], m + KD - 2)]
                    if use is not None:
                        s.wait_ge(v_evicted.sem, v_evicted.at(l, use + 1))
                    wait_unit(s, l, U_OF[it])
                    s.activation(gate_t[:, m % 2], bank[U_BANK[it] % 2][:, :], ACT.Tanh, scale=0.5
                                 ).then_inc(u_evicted.sem, 1)
                elif kind == "cstats":
                    for j in range(CN):
                        if j == 0:
                            s.wait_ge(u_evicted.sem, u_evicted.at(l, U_BANK[("in", "ckv", 0)] + 1))
                        square(l, latent[:, j], sq_at(0, 1) + KD + j)
                elif kind == "cnorm":
                    high_parts(l, h_at(0) + KD, yH[0], CN, None)
                elif kind == "uq":
                    wait_unit(s, l, U_OF[it])
                    for i in range(4):
                        s.activation(qC[0:NOPE, 4 * it[1] + i], bank[4 + i][0:NOPE, :], ACT.Copy, scale=-C_SCALE
                                     ).then_inc(qn_evicted.sem, 1)
                elif kind == "ukv":
                    for t in range(12):
                        if t < 11:
                            s.wait_ge(kv_done.sem, kv_done.at(l, t + 1))
                        else:
                            wait_unit(s, l, U_OF[it])
                        src = bank[4 + t % 4]
                        if t < HEADS:
                            s.activation(kC[0:NOPE, t], src[0:NOPE, :], ACT.Copy).then_inc(kv_evicted.sem, 1)
                        else:
                            s.activation(vC[:, t - HEADS], src[:, :], ACT.Copy).then_inc(kv_evicted.sem, 1)
                elif kind == "index":
                    b, h = it[1], it[2]
                    n = HEADS * (b - 1) + h
                    s.wait_ge(dots_ready.sem, dots_ready.at(l, n + 1))
                    if n >= 2:
                        s.wait_ge(index_added.sem, index_added.at(l, n - 1))
                    w = P * (b + 1)
                    s.activation(relu_sb[:, n % 2, 0:w], bank[4 + n % 2][:, 0:w], ACT.Relu
                                 ).then_inc(relu_ready.sem, 1)
                elif kind == "vtok":
                    n = {"A": 0, "D": 1}[it[1]]
                    s.wait_ge(vt_psum.sem, vt_psum.at(l, n + 1))
                    s.activation(v_tok[it[1]][:, :, :], bank[6][:, :].rearrange("p (t n) -> p t n", t=TB), ACT.Copy
                                 ).then_inc(vt_ready.sem, 1)
                elif kind == "att":
                    br, st = it[1], it[2]
                    if 1 <= st <= STEPS:
                        g = att_index(br, st - 1)
                        b, h, k0, nk = keys(br, st - 1)
                        s.wait_ge(pt_ready.sem, pt_ready.at(l, g + 1))
                        if g >= 2:
                            s.wait_ge(pv_done.sem, pv_done.at(l, g - 1))
                        s.activation(pt_sb[:, g % 2, 0:P * nk], bank[6][:, 0:P * nk], ACT.Copy
                                     ).then_inc(pt_evicted.sem, 1)
                    blk = (st - 10) // HEADS
                    if br == "D" and st >= 10 and (st - 10) % HEADS == 0 and blk < TB:
                        s.wait_ge(sink_sum.sem, sink_sum.at(l, blk + 1))
                        s.activation(skt[:, 8:16], skt[:, 0:8], ACT.Exp).then_inc(sink_exp.sem, 1)
                    if st < STEPS:
                        g = att_index(br, st)
                        b, h, k0, nk = keys(br, st)
                        c = 8 * (b % 2) + h
                        s.wait_ge(shifted.sem, shifted.at(l, g + 1))
                        s.activation(s_sb[:, g % 2, 0:P * nk], s_sb[:, g % 2, 0:P * nk], ACT.Exp, scale=-1.0,
                                     bias=nmax[:, c:c + 1], accum_out=rsum[:, c:c + 1]).then_inc(probs_ready.sem, 1)
                    blk = (st - 11) // HEADS
                    if st >= 11 and (st - 11) % HEADS == 0 and blk < TB:
                        g = TB * ATT.index(br) + blk
                        s.wait_ge(ytr_ready.sem, ytr_ready.at(l, g + 1))
                        use = V_BANK[("y", br, blk)]
                        s.activation(yH[Y_OF[br]][:, :, blk * P:(blk + 1) * P],
                                     bank[2 + use % 2][:, :].rearrange("p (t n) -> p t n", t=4), ACT.Copy
                                     ).then_inc(yhi_ready.sem, 1)
                elif kind == "lru":
                    j = it[1]
                    s.wait_ge(lru_psum.sem, lru_psum.at(l, j + 1))
                    if j >= 1:
                        s.wait_ge(lruv_ready.sem, lruv_ready.at(l, j))
                    s.activation(ti[:, :], bank[5][:, :], ACT.Tanh, scale=0.5, bias=hbx[:, j:j + 1]
                                 ).then_inc(ti_ready.sem, 1)
                    s.activation(tr[:, :], bank[4][:, :], ACT.Tanh, scale=0.5, bias=hba[:, j:j + 1])
                    s.drain()
                    s.activation(lru_a[:, j], tr[:, :], ACT.Exp, scale=nsp4[:, j:j + 1], bias=nsp4[:, j:j + 1])
                    s.drain()
                    s.activation(a_sq[:, :], lru_a[:, j], ACT.Square)
                    s.activation(tr[:, :], tr[:, :], ACT.Tanh, scale=sp4[:, j:j + 1], bias=sp4[:, j:j + 1]
                                 ).then_inc(asq_ready.sem, 1)
                    s.activation(lru_v[:, j], rg[:, j], ACT.Square).then_inc(rg_sq.sem, 1)
                    s.wait_ge(gelu_in.sem, gelu_in.at(l, j + 1))
                    s.activation(lru_v[:, j], lru_v[:, j], ACT.Tanh, scale=0.7978845608028654
                                 ).then_inc(gelu_t.sem, 1)
                elif kind == "sqrt":
                    s.wait_ge(lruv_ready.sem, lruv_ready.at(l, LRU_T))
                    s.activation(lru_v[:, :, :], lru_v[:, :, :], ACT.Sqrt).then_inc(sqrt_ready.sem, 1)
                elif kind == "scan":
                    j = it[1]
                    s.wait_ge(yb_ready.sem, yb_ready.at(l, j + 1))
                    s.activation(yH[Y_OF["B"]][:, j], lru_v[:, j], ACT.Copy).then_inc(yhi_ready.sem, 1)
                elif kind == "split_merged":
                    for m in range(KD):
                        if m == 0:
                            wait_unit(s, l, U_OF[("gate", "B", KD - 1)])
                        s.wait_ge(merged_ready.sem, merged_ready.at(l, m + 1))
                        s.activation(hH[:, m], merged[:, m], ACT.Copy).then_inc(mhi_ready.sem, 1)
                elif kind == "out":
                    m = it[1]
                    if 4 <= m < 8:
                        s.wait_ge(y_saved.sem, y_saved.at(l, 4 + m - 4 + 1))
                        square(l, y_half[:, m - 4], sq_at(1, 0) + m - 4)
                    if m == KD - 1:
                        wait_unit(s, l, U_OF[it])

        @block.scalar
        def _(s):
            def square(l, src, n, extra=None):
                s.wait_ge(sq_used.sem, sq_used.at(l, n - 1 if n else n))
                s.activation(sq[:, n % 2], src, ACT.Square).then_inc(sq_ready.sem, 1)

            def high_parts(l, n, dst, tiles, bias):
                for j in range(tiles):
                    s.wait_ge(u_ready.sem, u_ready.at(l, n + j + 1))
                    if bias is None:
                        s.activation(dst[:, j], tu[:, j % 2], ACT.Copy).then_inc(hh_ready.sem, 1)
                    else:
                        s.activation(dst[:, j], tu[:, j % 2], ACT.Identity, bias=bias(j)).then_inc(hh_ready.sem, 1)

            def shift_col(which):
                c = SLOT_OF[[3, 6, 0][which]]
                return lambda j: mod[:, c * KD + j:c * KD + j + 1]

            def end_of_boundary(l, n):
                for j in range(4, KD):
                    square(l, bank[j - 4][:, :], sq_at(n, 0) + j)
                s.wait_ge(bc_ready.sem, bc_ready.at(l, norm_at(n, 0) + 1))
                s.activation(rstd[:, :], bank[5][:, :], ACT.Copy).then_inc(rstd_ready.sem, 1)
                for j in range(KD):
                    s.wait_ge(x_ready.sem, x_ready.at(l, n * KD + j + 1))
                    square(l, x[:, j], sq_at(n, 1) + j)
                high_parts(l, h_at(n), hH, KD, shift_col(n))

            s.wait_ge(consts_in.sem, 16 * (5 + KD))
            s.activation(mod[:, 0:KD], ctmp[:, :], ACT.Tanh, scale=0.5).then_inc(c_tanh.sem, 1)
            for j in range(KD):
                if j >= 2:
                    s.wait_ge(sq_used.sem, j - 1)
                s.activation(sq[:, j % 2], x[:, j], ACT.Square).then_inc(sq_ready.sem, 1)
            for u in range(LEAD):
                s.wait_ge(raw_full[u].sem, 16)
                s.wait_ge(unit_done[u].sem, 1)
                s.activation(wH[:, u], raw[:, u], ACT.Copy).then_inc(hi_ready[u].sem, 1)
            high_parts(0, -KD, hH, KD, shift_col(2))

            with s.Fori(0, DEPTH) as l:
                for f in range(2):
                    u0 = U_FFN[f]

                    def turn(i):
                        for pp in range(2):
                            m = f * FT + 2 * i + pp
                            split_high(s, l, u0 + 2 * pp + LEAD, i)
                            wait_unit(s, l, u0 + 2 * pp, i)
                            s.wait_ge(pair_done.sem, pair_done.at(l, m - 1))
                            s.activation(tanh_g[:, pp], bank[2 * pp][:, :], ACT.Tanh, scale=0.5
                                         ).then_inc(gate_tanh.sem, 1)
                            split_high(s, l, u0 + 2 * pp + 1 + LEAD, i)
                            s.wait_ge(pair_done.sem, pair_done.at(l, m + 1))
                            s.activation(fH[:, bass.ds(2 * i + pp, 1), :], act[:, pp:pp + 1, :], ACT.Copy
                                         ).then_inc(ffn_hi.sem, 1)
                    with s.Fori(0, FT // 2) as i:
                        turn(i)
                    if f == 0:
                        s.wait_ge(sp_in.sem, sp_in.at(l, 1))
                        s.activation(lt[1][:, :], lt[0][:, :], ACT.Exp, scale=-1.0).then_inc(sp_exp.sem, 1)
                    n = 2 * f
                    for v in range(FT):
                        split_high(s, l, u0 + 2 * FT + v + LEAD)
                        if FT // 2 < v <= FT // 2 + 4:
                            j = v - FT // 2 - 1
                            s.wait_ge(y_saved.sem, y_saved.at(l, 4 * n + j + 1))
                            square(l, y_half[:, j], sq_at(n, 0) + j)
                    wait_unit(s, l, u0 + FFN_UNITS - 1)
                    end_of_boundary(l, n)
                    if f == 0:
                        scalar_mixer(s, l, split_high, square, high_parts)
                        end_of_boundary(l, 1)

        def pars_load(v, l):
            v.tensor_copy(parv[:, :], all_par[:, bass.ds(l, 1), :].rearrange("p a n -> p (a n)"))
            v.drain()

        def lru_parameters(v, l):
            lam = parv[:, PAR["lam"]:PAR["lam"] + LRU_T]
            v.scalar_tensor_tensor(lt[0][:, :], lam, -1.0, lam, ALU.mult, ALU.max).then_inc(sp_in.sem, 1)
            v.tensor_scalar(hba[:, :], parv[:, PAR["ba"]:PAR["ba"] + LRU_T], 0.5, None, ALU.mult)
            v.tensor_scalar(hbx[:, :], parv[:, PAR["bx"]:PAR["bx"] + LRU_T], 0.5, None, ALU.mult)
            v.tensor_scalar(nsink, nsink, -1.0, None, ALU.mult)
            v.wait_ge(sp_exp.sem, sp_exp.at(l, 1))
            v.tensor_scalar(lt[2][:, :], lt[1][:, :], 2.0, None, ALU.add)
            v.drain()
            v.reciprocal(lt[3][:, :], lt[2][:, :])
            v.drain()
            v.tensor_tensor(lt[1][:, :], lt[1][:, :], lt[3][:, :], ALU.mult)
            v.drain()
            v.tensor_tensor(lt[2][:, :], lt[1][:, :], lt[1][:, :], ALU.mult)
            v.drain()
            v.tensor_scalar(lt[3][:, :], lt[2][:, :], 1.0 / 19, 1.0 / 17, ALU.mult, ALU.add)
            for k in (15, 13, 11, 9, 7, 5, 3, 1):
                v.drain()
                v.tensor_tensor(lt[3][:, :], lt[3][:, :], lt[2][:, :], ALU.mult)
                v.drain()
                v.tensor_scalar(lt[3][:, :], lt[3][:, :], 1.0 / k, None, ALU.add)
            v.drain()
            v.tensor_tensor(lt[3][:, :], lt[3][:, :], lt[1][:, :], ALU.mult)
            v.tensor_scalar(lt[2][:, :], lam, -1.0, 0.0, ALU.mult, ALU.max)
            v.drain()
            v.scalar_tensor_tensor(lt[3][:, :], lt[3][:, :], 2.0, lt[2][:, :], ALU.mult, ALU.add)
            v.drain()
            v.tensor_scalar(sp4[:, :], lt[3][:, :], 4.0, None, ALU.mult)
            v.tensor_scalar(nsp4[:, :], lt[3][:, :], -4.0, None, ALU.mult).then_inc(lru_params.sem, 1)

        def vector_mixer(v, l, diagonal, normalise, save_half):
            for it in MIXER:
                kind = it[0]
                if kind in UNIT_KINDS:
                    split_low(v, l, U_OF[it] + LEAD)
                v.drain()
                if kind == "in" and it[1] == "rx" and it[2] == 0:
                    v.wait_ge(pv_done.sem, pv_done.at(l, 2 * STEPS))
                    v.memset(rx[:, :, 0:PAD], 0.0).then_inc(pads_ready.sem, 1)
                elif kind == "cstats":
                    v.wait_ge(sq_used.sem, sq_used.at(l, 2 * KD + CN))
                    v.tensor_scalar(ms[:, 0:TB], bank[7][:, 0:TB], 1.0 / 256, EPS, ALU.mult, ALU.add)
                    v.drain()
                    v.tensor_scalar(ms[:, TB:2 * TB], bank[7][:, 8:8 + TB], 1.0 / P, EPS, ALU.mult, ALU.add
                                    ).then_inc(ms_ready.sem, 1)
                elif kind == "cbcast":
                    v.wait_ge(rs_ready.sem, rs_ready.at(l, 3))
                    diagonal(l, 2, diag2[:, 0], 0)
                    v.drain()
                    diagonal(l, 2, diag2[:, 1], TB).then_inc(diag_ready.sem, 1)
                elif kind == "cnorm":
                    v.wait_ge(bc_ready.sem, bc_ready.at(l, 3))
                    g = PAR["g_q"]
                    normalise(l, h_at(0) + KD, lambda j: latent[:, j], lambda j: parv[:, g + j:g + j + 1],
                              lambda j: bank[5 + j // 2][:, :], yH[0], yL[0], CN, None)
                elif kind == "uq":
                    v.wait_ge(mixc_in.sem, mixc_in.at(l, 16))
                    wait_unit(v, l, U_OF[it])
                    for i in range(4):
                        h = 4 * it[1] + i
                        v.tensor_tensor(krope[64:96, :], bank[4 + i][96:128, :], rope_q[96:128, :], ALU.mult)
                        v.tensor_tensor(qC[64:96, h], bank[4 + i][64:96, :], rope_q[64:96, :], ALU.mult)
                        v.drain()
                        v.tensor_tensor(qC[64:96, h], qC[64:96, h], krope[64:96, :], ALU.add
                                        ).then_inc(qr_evicted.sem, 1)
                        v.drain()
                elif kind == "ukv":
                    v.drain()
                    v.wait_ge(u_evicted.sem, u_evicted.at(l, U_BANK[("in", "misc", 0)] + 1))
                    v.tensor_tensor(kC[64:96, 0], misc[64:96, :], rope_k[64:96, :], ALU.mult)
                    v.tensor_tensor(kC[64:96, 1], misc[96:128, :], rope_k[96:128, :], ALU.mult)
                    v.drain()
                    v.tensor_tensor(kC[64:96, 2], kC[64:96, 0], kC[64:96, 1], ALU.add)
                    v.drain()
                    v.tensor_copy(kC[64:96, 0:2, :], kC[64:96, 2:3, :].broadcast_to([32, 2, T]))
                    v.tensor_copy(kC[64:96, 3:HEADS, :], kC[64:96, 2:3, :].broadcast_to([32, HEADS - 3, T])
                                  ).then_inc(kr_ready.sem, 1)
                elif kind == "wi":
                    v.wait_ge(wi_psum.sem, wi_psum.at(l, 1))
                    v.tensor_copy(wi[:, :].rearrange("p (t h) -> p t h", t=TB),
                                  bank[6][:, :].rearrange("p (t n) -> p t n", t=TB)[:, :, 0:8]).then_inc(wi_ready.sem, 1)
                    v.drain()
                elif kind == "index":
                    b, h = it[1], it[2]
                    n = HEADS * (b - 1) + h
                    w = P * (b + 1)
                    c = 8 * b + h
                    if h > 0:
                        v.drain()
                    v.wait_ge(relu_ready.sem, relu_ready.at(l, n + 1))
                    if h == 0:
                        v.tensor_scalar(pick[b][:, :], relu_sb[:, n % 2, 0:w], wi[:, c:c + 1], None, ALU.mult
                                        ).then_inc(index_added.sem, 1)
                    else:
                        v.scalar_tensor_tensor(pick[b][:, :], relu_sb[:, n % 2, 0:w], wi[:, c:c + 1], pick[b][:, :],
                                               ALU.mult, ALU.add).then_inc(index_added.sem, 1)
                    if h == HEADS - 1:
                        v.drain()
                        v.scalar_tensor_tensor(pick[b][:, w - P:w], causal[:, T - P:T], -1e8, pick[b][:, w - P:w],
                                               ALU.mult, ALU.add)
                elif kind == "topk":
                    b, r = it[1], it[2]
                    v.drain()
                    v.max(top8[:, :], pick[b][:, :])
                    v.drain()
                    v.match_replace(pick[b][:, :], top8[:, :], pick[b][:, :], -3e38)
                    if r == TOPK // 8 - 1:
                        v.drain()
                        v.tensor_scalar(pick[b][:, :], pick[b][:, :], -2e38, BIG, ALU.is_gt, ALU.mult)
                elif kind == "att":
                    vector_attention(v, l, it[1], it[2])
                elif kind == "branch":
                    n, mp = it[1], it[2]
                    wait_unit(v, l, U_OF[it])
                    for m in (2 * mp, 2 * mp + 1):
                        gate = gate_t[:, m % 2]
                        v.wait_ge(u_evicted.sem, u_evicted.at(l, U_BANK[("gate", n, m)] + 1))
                        src = bank[2 + V_BANK[("proj", n, m)] % 2][:, :]
                        if n == BRANCHES[0]:
                            v.scalar_tensor_tensor(merged[:, m], gate, 1.0, src, ALU.add, ALU.mult
                                                   ).then_inc(v_evicted.sem, 1)
                        else:
                            v.scalar_tensor_tensor(gated[:, m % 2], gate, 1.0, src, ALU.add, ALU.mult
                                                   ).then_inc(v_evicted.sem, 1)
                            v.drain()
                            op = v.tensor_tensor(merged[:, m], merged[:, m], gated[:, m % 2], ALU.add)
                            if n == BRANCHES[-1]:
                                op.then_inc(merged_ready.sem, 1)
                elif kind == "conv":
                    j = it[1]
                    w0 = PAR["conv_w"] + 4 * j
                    v.drain()
                    if j == 0:
                        v.wait_ge(u_evicted.sem, u_evicted.at(l, U_BANK[("in", "rg", LRU_T - 1)] + 1))
                    v.tensor_scalar(xc[:, :], rx[:, j, 0:T], parv[:, w0:w0 + 1],
                                    parv[:, PAR["conv_b"] + j:PAR["conv_b"] + j + 1], ALU.mult, ALU.add)
                    for k in range(1, 4):
                        v.drain()
                        op = v.scalar_tensor_tensor(xc[:, :], rx[:, j, k:k + T], parv[:, w0 + k:w0 + k + 1],
                                                    xc[:, :], ALU.mult, ALU.add)
                    op.then_inc(conv_ready.sem, 1)
                elif kind == "lru":
                    j = it[1]
                    v.drain()
                    v.wait_ge(ti_ready.sem, ti_ready.at(l, j + 1))
                    v.scalar_tensor_tensor(ix[:, j, 0:T], ti[:, :], 1.0, xc[:, :], ALU.add, ALU.mult)
                    v.wait_ge(rg_sq.sem, rg_sq.at(l, j + 1))
                    v.tensor_scalar(lru_v[:, j], lru_v[:, j], 0.044715, 1.0, ALU.mult, ALU.add)
                    v.drain()
                    v.tensor_tensor(lru_v[:, j], lru_v[:, j], rg[:, j], ALU.mult).then_inc(gelu_in.sem, 1)
                    v.wait_ge(gelu_t.sem, gelu_t.at(l, j + 1))
                    v.scalar_tensor_tensor(rg[:, j], lru_v[:, j], 1.0, rg[:, j], ALU.add, ALU.mult)
                    v.drain()
                    v.wait_ge(asq_ready.sem, asq_ready.at(l, j + 1))
                    v.scalar_tensor_tensor(lru_v[:, j], a_sq[:, :], 1.0, tr[:, :], ALU.add, ALU.mult
                                           ).then_inc(lruv_ready.sem, 1)
                elif kind == "scan":
                    j = it[1]
                    v.drain()
                    if j == 0:
                        v.wait_ge(sqrt_ready.sem, sqrt_ready.at(l, 1))
                    v.tensor_tensor(ix[:, j, 0:T], ix[:, j, 0:T], lru_v[:, j], ALU.mult)
                    v.drain()
                    v.tensor_tensor_scan(lru_v[:, j], lru_a[:, j], ix[:, j, 0:T], 0.0, ALU.mult, ALU.add)
                    v.drain()
                    v.scalar_tensor_tensor(lru_v[:, j], lru_v[:, j], 0.25, rg[:, j], ALU.mult, ALU.mult
                                           ).then_inc(yb_ready.sem, 1)
                    v.drain()
                    v.wait_ge(yhi_ready.sem, yhi_ready.at(l, TB * len(ATT) + j + 1))
                    v.tensor_tensor(yL[Y_OF["B"]][:, j], lru_v[:, j], yH[Y_OF["B"]][:, j].bitcast(F32), ALU.subtract
                                    ).then_inc(yb_lo.sem, 1)
                elif kind == "split_merged":
                    for m in range(KD):
                        v.wait_ge(mhi_ready.sem, mhi_ready.at(l, m + 1))
                        op = v.tensor_tensor(hL[:, m], merged[:, m], hH[:, m].bitcast(F32), ALU.subtract)
                        op.then_inc(mlo_ready.sem, 1)
                elif kind == "out" and it[1] >= 4:
                    if it[1] == 4:
                        v.drain()
                        wait_unit(v, l, U_OF[("out", 3)])
                    save_half(l, 1, it[1] - 4)

        def vector_attention(v, l, br, st):
            blk = (st - 10) // HEADS
            if st >= 10 and (st - 10) % HEADS == 0 and blk < TB:
                cols = slice(8 * (blk % 2), 8 * (blk % 2) + 8)
                g = TB * ATT.index(br) + blk
                v.drain()
                v.wait_ge(pv_done.sem, pv_done.at(l, att_index(br, HEADS * blk + HEADS - 1) + 1))
                if br == "D":
                    v.tensor_tensor(skt[:, 0:8], nmax[:, cols], nsink, ALU.subtract
                                    ).then_inc(sink_sum.sem, 1)
                    v.wait_ge(sink_exp.sem, sink_exp.at(l, blk + 1))
                    v.tensor_tensor(rsum[:, cols], rsum[:, cols], skt[:, 8:16], ALU.add)
                    v.drain()
                v.reciprocal(recip[:, :], rsum[:, cols])
                v.drain()
                if g >= 1:
                    v.wait_ge(ytr_ready.sem, ytr_ready.at(l, g))
                v.tensor_tensor(y_tok[:, :].rearrange("p (h d) -> p h d", h=HEADS),
                                bank[7][:, :].rearrange("p (h d) -> p h d", h=HEADS),
                                recip[:, :, None].broadcast_to([P, HEADS, HD]), ALU.mult).then_inc(ytok_ready.sem, 1)
            if st < STEPS:
                g = att_index(br, st)
                b, h, k0, nk = keys(br, st)
                w = P * nk
                if br == "C":
                    bias = causal[:, T - w:T]
                else:
                    if br == "D":
                        mask = window[:, 2 * P - w:2 * P]
                    else:
                        mask = causal[:, T - P:T] if b == 0 else pick[b][:, :]
                    bias = bias_sb[:, 0:w]
                v.drain()
                if g >= 2:
                    v.wait_ge(pt_ready.sem, pt_ready.at(l, g - 1))
                v.wait_ge(scores_ready.sem, scores_ready.at(l, g + 1))
                if br == "C":
                    v.sem_inc(scores_seen.sem, 1)
                else:
                    v.scalar_tensor_tensor(bias, dist[:, T - w:T], SLOPE[br][h], mask, ALU.mult, ALU.add)
                    v.drain()
                c = 8 * (b % 2) + h
                first = nsink[:, h:h + 1] if br == "D" else 3e38
                v.tensor_tensor_reduce(s_sb[:, g % 2, 0:w], bank[4 + g % 2][:, 0:w], bias, 1.0, first, ALU.add,
                                       ALU.min, nmax[:, c:c + 1]).then_inc(shifted.sem, 1)
            blk = (st - 11) // HEADS
            if st >= 11 and (st - 11) % HEADS == 0 and blk < TB:
                g = TB * ATT.index(br) + blk
                v.wait_ge(yhi_ready.sem, yhi_ready.at(l, g + 1))
                cols = slice(blk * P, (blk + 1) * P)
                use = V_BANK[("y", br, blk)]
                i = Y_OF[br]
                v.tensor_tensor(yL[i][:, :, cols], bank[2 + use % 2][:, :].rearrange("p (t n) -> p t n", t=4),
                                yH[i][:, :, cols].bitcast(F32), ALU.subtract).then_inc(v_evicted.sem, 1)

        @block.vector
        def _(v):
            def mean_square(l, n, cols, width, size, eps, inc=True):
                op = v.tensor_scalar(ms[:, cols:cols + TB], bank[4][:, width:width + TB], 1.0 / size, eps,
                                     ALU.mult, ALU.add)
                return op

            def diagonal(l, n, dst, col):
                return v.tensor_tensor(dst, ident[:, None, :].broadcast_to([P, TB, P]),
                                       rs[:, col:col + TB][:, :, None].broadcast_to([P, TB, P]), ALU.mult)

            def normalise(l, n, src, scale, bc, dst_h, dst_l, tiles, bias):
                def low(j):
                    v.wait_ge(hh_ready.sem, hh_ready.at(l, n + j + 1))
                    if bias is None:
                        v.tensor_tensor(dst_l[:, j], tu[:, j % 2], dst_h[:, j].bitcast(F32), ALU.subtract
                                        ).then_inc(h_ready.sem, 1)
                    else:
                        v.scalar_tensor_tensor(dst_l[:, j], tu[:, j % 2], bias(j), dst_h[:, j].bitcast(F32),
                                               ALU.add, ALU.subtract).then_inc(h_ready.sem, 1)
                for j in range(tiles):
                    if j >= 2:
                        v.drain()
                    v.scalar_tensor_tensor(tu[:, j % 2], src(j), scale(j), bc(j), ALU.mult, ALU.mult
                                           ).then_inc(u_ready.sem, 1)
                    if j >= 1:
                        low(j - 1)
                low(tiles - 1)
                v.drain()

            def shift_col(which):
                c = SLOT_OF[[3, 6, 0][which]]
                return lambda j: mod[:, c * KD + j:c * KD + j + 1]

            def pre_vector(which):
                c = SLOT_OF[[4, 7, 1][which]] * KD
                g = PAR["norm_g"] + [2, 4, 0][which] * KD
                v.scalar_tensor_tensor(vecA[:, :], mod[:, c:c + KD], 1.0, parv[:, g:g + KD], ALU.add, ALU.mult)

            def vectors(which):
                c = SLOT_OF[[2, 5, 8][which]] * KD
                g = PAR["norm_g"] + [1, 3, 5][which] * KD
                v.scalar_tensor_tensor(vecC[:, :], mod[:, c:c + KD], [0.5, 1.0, 0.5][which], parv[:, g:g + KD],
                                       ALU.mult, ALU.mult)
                pre_vector(which)

            def save_half(l, n, j):
                v.tensor_copy(y_half[:, j], bank[4 + j][:, :]).then_inc(y_saved.sem, 1)

            def end_of_boundary(l, n):
                v.drain()
                vectors(n)
                v.drain()
                v.wait_ge(sq_used.sem, sq_used.at(l, sq_at(n, 0) + KD))
                mean_square(l, n, 0, 0, D, 4 * EPS).then_inc(ms_ready.sem, 1)
                v.wait_ge(rs_ready.sem, rs_ready.at(l, norm_at(n, 0) + 1))
                diagonal(l, n, diag[:, :, :], 0).then_inc(diag_ready.sem, 1)
                v.wait_ge(rstd_ready.sem, rstd_ready.at(l, n + 1))
                for j in range(0, KD, 2):
                    for jj in (j, j + 1):
                        y = y_half[:, jj] if jj < 4 else bank[jj - 4][:, :]
                        v.scalar_tensor_tensor(tu[:, jj % 2], y, vecC[:, jj:jj + 1], rstd[:, :], ALU.mult, ALU.mult)
                    v.drain()
                    for jj in (j, j + 1):
                        v.tensor_tensor(x[:, jj], x[:, jj], tu[:, jj % 2], ALU.add).then_inc(x_ready.sem, 1)
                    v.drain()
                pre_norm(l, n)

            def pre_norm(l, n):
                v.wait_ge(sq_used.sem, sq_used.at(l, sq_at(n, 1) + KD))
                mean_square(l, n, 0, 8, D, EPS).then_inc(ms_ready.sem, 1)
                v.wait_ge(rs_ready.sem, rs_ready.at(l, norm_at(n, 1) + 1))
                diagonal(l, n, diag[:, :, :], 0).then_inc(diag_ready.sem, 1)
                v.wait_ge(bc_ready.sem, bc_ready.at(l, norm_at(n, 1) + 1))
                normalise(l, h_at(n), lambda j: x[:, j], lambda j: vecA[:, j:j + 1], lambda j: bank[6][:, :], hH, hL,
                          KD, shift_col(n))

            def ada_step(s):
                if s == 0:
                    v.tensor_scalar(ada_acc[:, :], ada_raw[:, 0], cs[:, 0:1], None, ALU.mult
                                    ).then_inc(ada_used.sem, 1)
                else:
                    v.scalar_tensor_tensor(ada_acc[:, :], ada_raw[:, s % 2], cs[:, s:s + 1], ada_acc[:, :],
                                           ALU.mult, ALU.add).then_inc(ada_used.sem, 1)

            for slot in range(RING):
                v.sem_inc(lo_ready[slot].sem, 1)
            v.sem_inc(ada_used.sem, 2)
            v.sem_inc(ada_sum.sem, 1)
            v.sem_inc(pair_done.sem, 2)
            v.sem_inc(ffn_lo.sem, 2)
            v.sem_inc(u_evicted.sem, 2)
            v.sem_inc(v_evicted.sem, 2)
            v.wait_ge(c_tanh.sem, 1)
            v.scalar_tensor_tensor(cs[:, :], mod[:, 0:KD], 1.0, ctmp[:, :], ALU.add, ALU.mult)
            v.drain()
            v.tensor_scalar(cs[:, :], cs[:, :], 0.5, None, ALU.mult)
            for c in range(2):
                v.drain()
                v.wait_ge(ada_sum.sem, c + 1)
                for s in range(8):
                    if s > 0:
                        v.drain()
                    v.wait_ge(ada_full[s % 2].sem, 16 * (4 * c + s // 2 + 1))
                    ada_step(s)
                v.wait_ge(ada_sum.sem, c + 2)
                v.tensor_tensor(mod[:, (7 + c) * KD:(8 + c) * KD], bank[7][:, 0:KD], parv[:, c * KD:(c + 1) * KD],
                                ALU.add).then_inc(mod_ready.sem, 1)
            v.drain()
            v.scalar_tensor_tensor(vecA[:, :], mod[:, 8 * KD:9 * KD], 1.0, parv[:, 2 * KD:3 * KD], ALU.add, ALU.mult)
            v.wait_ge(sq_used.sem, KD)
            v.tensor_scalar(ms[:, 0:TB], bank[4][:, 8:8 + TB], 1.0 / D, EPS, ALU.mult, ALU.add
                            ).then_inc(ms_ready.sem, 1)
            for u in range(LEAD):
                v.wait_ge(hi_ready[u].sem, 1)
                v.tensor_tensor(wL[:, u], raw[:, u], wH[:, u].bitcast(F32), ALU.subtract
                                ).then_inc(lo_ready[u].sem, 1)
            v.wait_ge(rs_ready.sem, 1)
            diagonal(0, 0, diag[:, :, :], 0).then_inc(diag_ready.sem, 1)
            v.wait_ge(bc_ready.sem, 1)
            normalise(0, -KD, lambda j: x[:, j], lambda j: vecA[:, j:j + 1], lambda j: bank[6][:, :], hH, hL, KD,
                      shift_col(2))
            v.sem_inc(ada_free.sem, 1)

            with v.Fori(0, DEPTH) as l:
                v.drain()
                pars_load(v, l)
                for f in range(2):
                    u0 = U_FFN[f]

                    def turn(i, ada_on):
                        c = 7 * f + i

                        def steps(group):
                            if ada_on:
                                if group == 0:
                                    v.wait_ge(ada_sum.sem, ada_sum.at(l, c))
                                for s in (2 * group, 2 * group + 1):
                                    if s > 0:
                                        v.drain()
                                    full = ada_full[s % 2]
                                    v.wait_ge(full.sem, full.at(l, 16 * (4 * c + s // 2 + 1)))
                                    ada_step(s)
                        for pp in range(2):
                            m = f * FT + 2 * i + pp
                            split_low(v, l, u0 + 2 * pp + LEAD, i)
                            steps(2 * pp)
                            v.wait_ge(ffn_lo.sem, ffn_lo.at(l, m - 1))
                            v.wait_ge(gate_tanh.sem, gate_tanh.at(l, m + 1))
                            v.scalar_tensor_tensor(act[:, pp], tanh_g[:, pp], 1.0, bank[2 * pp][:, :], ALU.add,
                                                   ALU.mult)
                            split_low(v, l, u0 + 2 * pp + 1 + LEAD, i)
                            steps(2 * pp + 1)
                            v.drain()
                            wait_unit(v, l, u0 + 2 * pp + 1, i)
                            v.tensor_tensor(act[:, pp], act[:, pp], bank[2 * pp + 1][:, :], ALU.mult
                                            ).then_inc(pair_done.sem, 1)
                        if ada_on:
                            v.wait_ge(ada_sum.sem, ada_sum.at(l, c + 1))
                            v.tensor_tensor(mod[:, bass.ds(c * KD, KD)], bank[7][:, 0:KD],
                                            parv[:, bass.ds(PAR["b_ada"] + c * KD, KD)], ALU.add
                                            ).then_inc(mod_ready.sem, 1)
                    with v.Fori(0, ADA_FFN[f]) as i:
                        turn(i, True)
                    with v.Fori(ADA_FFN[f], FT // 2) as i:
                        turn(i, False)
                    if f == 0:
                        lru_parameters(v, l)
                    n = 2 * f
                    for q in range(FT):
                        split_low(v, l, u0 + 2 * FT + q + LEAD)
                        if FT // 2 < q <= FT // 2 + 4:
                            j = q - FT // 2 - 1
                            if j == 0:
                                wait_unit(v, l, u0 + 2 * FT + FT // 2 - 1)
                            save_half(l, n, j)
                    end_of_boundary(l, n)
                    if f == 0:
                        vector_mixer(v, l, diagonal, normalise, save_half)
                        end_of_boundary(l, 1)
                    v.sem_inc(ada_free.sem, 1)
            v.drain()

        def tensor_mixer(pe, l, sum_squares, spread):
            first_in = True
            for it in MIXER:
                kind = it[0]
                if kind in ("in", "gate"):
                    slot = unit_ready(pe, l, U_OF[it])
                    c = U_BANK[it]
                    pe.wait_ge(u_evicted.sem, u_evicted.at(l, c - 1))
                    for k in range(KD):
                        if first_in:
                            pe.wait_ge(h_ready.sem, h_ready.at(l, h_at(0) + k + 1))
                        mm = product(pe, bank[c % 2][:, :], slot, k * P, slice(0, P), hH[:, k], hL[:, k], k == 0,
                                     k == KD - 1)
                    first_in = False
                    mm.then_inc(unit_done[slot].sem, 1)
                elif kind == "cstats":
                    n0 = sq_at(0, 1) + KD
                    for j in range(CN):
                        sum_squares(l, n0 + j, 8 if j == 2 else 0, j == 0, 7)
                elif kind == "cbcast":
                    pe.wait_ge(diag_ready.sem, diag_ready.at(l, 3))
                    for i in range(2):
                        spread(l, 2, diag2[:, i].rearrange("p t n -> p (t n)"), 5 + i, i == 1)
                elif kind == "uq":
                    slot = unit_ready(pe, l, U_OF[it])
                    if it[1] == 0:
                        pe.wait_ge(h_ready.sem, h_ready.at(l, h_at(0) + KD + CN))
                    else:
                        pe.wait_ge(qn_evicted.sem, qn_evicted.at(l, 4))
                        pe.wait_ge(qr_evicted.sem, qr_evicted.at(l, 4))
                    for i in range(4):
                        for k in range(2):
                            mm = product(pe, bank[4 + i][:, :], slot, (2 * i + k) * P, slice(0, P), yH[0][:, k],
                                         yL[0][:, k], k == 0, k == 1)
                    mm.then_inc(unit_done[slot].sem, 1)
                elif kind == "ukv":
                    slot = unit_ready(pe, l, U_OF[it])
                    for t in range(12):
                        if t < 4:
                            if t == 0:
                                pe.wait_ge(qn_evicted.sem, qn_evicted.at(l, HEADS))
                                pe.wait_ge(qr_evicted.sem, qr_evicted.at(l, HEADS))
                        else:
                            pe.wait_ge(kv_evicted.sem, kv_evicted.at(l, t - 3))
                        o = bank[4 + t % 4]
                        if t < HEADS:
                            mm = product(pe, o[:, :], slot, NOPE * t, slice(0, P), yH[0][:, 2], yL[0][:, 2],
                                         True, True)
                        else:
                            tb = slice((t - HEADS) * P, (t - HEADS + 1) * P)
                            vh, vl = wH[:, slot, T:2 * T], wL[:, slot, T:2 * T]
                            pe.matmul(o[:, :], yH[0][:, 2, tb], vh, start=True, stop=False)
                            pe.matmul(o[:, :], yL[0][:, 2, tb], vh, start=False, stop=False)
                            mm = pe.matmul(o[:, :], yH[0][:, 2, tb], vl, start=False, stop=True)
                        mm.then_inc(kv_done.sem if t < 11 else unit_done[slot].sem, 1)
                elif kind == "wi":
                    pe.wait_ge(kv_evicted.sem, kv_evicted.at(l, 12))
                    for tb in range(TB):
                        mm = pe.transpose(bank[6][:, tb * P:(tb + 1) * P], misc[:, tb * P:(tb + 1) * P], ident[:, :])
                    mm.then_inc(wi_psum.sem, 1)
                elif kind == "index":
                    b, h = it[1], it[2]
                    n = HEADS * (b - 1) + h
                    if n >= 2:
                        pe.wait_ge(relu_ready.sem, relu_ready.at(l, n - 1))
                    if n == 0:
                        pe.wait_ge(u_evicted.sem, u_evicted.at(l, U_BANK[("in", "ik", 0)] + 1))
                    rows = slice(64 * (h % 2), 64 * (h % 2) + 64)
                    pe.matmul(bank[4 + n % 2][:, 0:P * (b + 1)], iq[rows, h // 2, b * P:(b + 1) * P],
                              ik[rows, 0:P * (b + 1)], start=True, stop=True).then_inc(dots_ready.sem, 1)
                elif kind == "vtok":
                    br = it[1]
                    src = {"A": av, "D": dv}[br]
                    pe.wait_ge(u_evicted.sem, u_evicted.at(l, U_BANK[("in", {"A": "av", "D": "dv"}[br], 0)] + 1))
                    pe.wait_ge(pt_evicted.sem, pt_evicted.at(l, STEPS * (1 if br == "A" else 2)))
                    for tb in range(TB):
                        mm = pe.transpose(bank[6][:, tb * P:(tb + 1) * P], src[:, tb * P:(tb + 1) * P], ident[:, :])
                    mm.then_inc(vt_psum.sem, 1)
                elif kind == "att":
                    tensor_attention(pe, l, it[1], it[2])
                elif kind == "branch":
                    n, mp = it[1], it[2]
                    slot = unit_ready(pe, l, U_OF[it])
                    i = Y_OF[n]
                    y_done = V_BANK.get(("y", n, TB - 1), 0) + 1
                    if mp == 0 and n == "B":
                        pe.wait_ge(yb_lo.sem, yb_lo.at(l, LRU_T))
                    for m in range(2):
                        use = V_BANK[("proj", n, 2 * mp + m)]
                        pe.wait_ge(v_evicted.sem, v_evicted.at(l, max(use - 1, y_done)))
                        for k in range(4):
                            mm = product(pe, bank[2 + use % 2][:, :], slot, (4 * m + k) * P, slice(0, P), yH[i][:, k],
                                         yL[i][:, k], k == 0, k == 3)
                    mm.then_inc(unit_done[slot].sem, 1)
                elif kind == "lru":
                    j = it[1]
                    pe.wait_ge(conv_ready.sem, conv_ready.at(l, j + 1))
                    if j == 0:
                        pe.wait_ge(lru_in.sem, lru_in.at(l, 16))
                    else:
                        pe.wait_ge(asq_ready.sem, asq_ready.at(l, j))
                    pe.matmul(bank[4][:, :], lru_w[:, j], xc[:, :], start=True, stop=True)
                    pe.matmul(bank[5][:, :], lru_w[:, LRU_T + j], xc[:, :], start=True, stop=True
                              ).then_inc(lru_psum.sem, 1)
                elif kind == "out":
                    m = it[1]
                    slot = unit_ready(pe, l, U_OF[it])
                    o = bank[4 + m if m < 4 else m - 4]
                    if m == 0:
                        pe.wait_ge(ytok_ready.sem, ytok_ready.at(l, TB * len(ATT)))
                        pe.wait_ge(asq_ready.sem, asq_ready.at(l, LRU_T))
                    if m == 4:
                        pe.wait_ge(v_evicted.sem, v_evicted.at(l, V_USES))
                        pe.wait_ge(u_evicted.sem, u_evicted.at(l, len(U_BANK)))
                    for k in range(KD):
                        if m == 0:
                            pe.wait_ge(mlo_ready.sem, mlo_ready.at(l, k + 1))
                        mm = product(pe, o[:, :], slot, k * P, slice(0, P), hH[:, k], hL[:, k], k == 0, k == KD - 1)
                    mm.then_inc(unit_done[slot].sem, 1)
                    if m >= 4:
                        if m == 4:
                            pe.wait_ge(y_saved.sem, y_saved.at(l, 4 + 1))
                        sum_squares(l, sq_at(1, 0) + m - 4, 0, m == 4)

        def tensor_attention(pe, l, br, st):
            if st < STEPS:
                g = att_index(br, st)
                b, h, k0, nk = keys(br, st)
                if st == 0:
                    if br == "C":
                        pe.wait_ge(relu_ready.sem, relu_ready.at(l, NI))
                        pe.wait_ge(kr_ready.sem, kr_ready.at(l, 1))
                    elif br == "A":
                        pe.wait_ge(u_evicted.sem, u_evicted.at(l, U_BANK[("in", "ak", 0)] + 1))
                    else:
                        pe.wait_ge(u_evicted.sem, u_evicted.at(l, U_BANK[("in", "dk", 0)] + 1))
                if g >= 2:
                    pe.wait_ge(shifted.sem, shifted.at(l, g - 1))
                q = slice(b * P, (b + 1) * P)
                kk = slice(k0 * P, (k0 + nk) * P)
                if br == "C":
                    a, c = qC[0:96, h, q], kC[0:96, h, kk]
                else:
                    rows = slice(64 * (h // 4), 64 * (h // 4) + 64)
                    qq, kx = (aq, ak) if br == "A" else (dq, dk)
                    a, c = qq[rows, h % 4, q], kx[rows, kk]
                pe.matmul(bank[4 + g % 2][:, 0:P * nk], a, c, start=True, stop=True).then_inc(scores_ready.sem, 1)
            if 1 <= st <= STEPS:
                g = att_index(br, st - 1)
                b, h, k0, nk = keys(br, st - 1)
                pe.wait_ge(probs_ready.sem, probs_ready.at(l, g + 1))
                if g >= 1:
                    pe.wait_ge(pt_evicted.sem, pt_evicted.at(l, g))
                if g == STEPS or g == 2 * STEPS:
                    pe.wait_ge(vt_ready.sem, vt_ready.at(l, g // STEPS))
                for i in range(nk):
                    mm = pe.transpose(bank[6][:, i * P:(i + 1) * P], s_sb[:, g % 2, i * P:(i + 1) * P], ident[:, :])
                mm.then_inc(pt_ready.sem, 1)
            if 2 <= st <= STEPS + 1:
                g = att_index(br, st - 2)
                b, h, k0, nk = keys(br, st - 2)
                pe.wait_ge(pt_evicted.sem, pt_evicted.at(l, g + 1))
                if h == 0 and g > 0:
                    pe.wait_ge(ytok_ready.sem, ytok_ready.at(l, g // HEADS))
                for i in range(nk):
                    vv = vC[:, k0 + i, h * HD:(h + 1) * HD] if br == "C" else \
                        v_tok[br][:, k0 + i, (h // 4) * HD:(h // 4 + 1) * HD]
                    mm = pe.matmul(bank[7][:, h * HD:(h + 1) * HD], pt_sb[:, g % 2, i * P:(i + 1) * P], vv,
                                   start=i == 0, stop=i == nk - 1)
                mm.then_inc(pv_done.sem, 1)
            blk = (st - 11) // HEADS
            if st >= 11 and (st - 11) % HEADS == 0 and blk < TB:
                g = TB * ATT.index(br) + blk
                pe.wait_ge(ytok_ready.sem, ytok_ready.at(l, g + 1))
                use = V_BANK[("y", br, blk)]
                pe.wait_ge(v_evicted.sem, v_evicted.at(l, use - 1))
                for t in range(4):
                    mm = pe.transpose(bank[2 + use % 2][:, t * P:(t + 1) * P], y_tok[:, t * P:(t + 1) * P],
                                      ident[:, :])
                mm.then_inc(ytr_ready.sem, 1)

        @block.tensor
        def _(pe):
            def sum_squares(l, n, col, first, b=4, i=0):
                pe.wait_ge(sq_ready.sem, sq_ready.at(l, n + 1))
                for tb in range(TB):
                    mm = pe.matmul(bank[b][:, col + tb:col + tb + 1], sq[:, n % 2, tb * P:(tb + 1) * P], ones[:, 0:1],
                                   start=first and tb == 0, stop=True, skip_group_check=True)
                mm.then_inc(sq_used.sem, 1)

            def spread(l, n, src, b, inc=True):
                mm = pe.matmul(bank[b][:, :], ones[:, :], src, start=True, stop=True)
                if inc:
                    mm.then_inc(bc_ready.sem, 1)

            def end_of_boundary(l, n):
                for j in range(4, KD):
                    sum_squares(l, sq_at(n, 0) + j, 0, False)
                pe.wait_ge(diag_ready.sem, diag_ready.at(l, norm_at(n, 0) + 1))
                spread(l, n, diag[:, :, :].rearrange("p t n -> p (t n)"), 5)
                for j in range(KD):
                    sum_squares(l, sq_at(n, 1) + j, 8, j == 0)
                pe.wait_ge(diag_ready.sem, diag_ready.at(l, norm_at(n, 1) + 1))
                spread(l, n, diag[:, :, :].rearrange("p t n -> p (t n)"), 6)

            def ada_sums():
                for j in range(KD):
                    mm = pe.matmul(bank[7][:, j:j + 1], ada_acc[:, j * P:(j + 1) * P], ones[:, 0:1], start=j == 0,
                                   stop=True, skip_group_check=True)
                mm.then_inc(ada_sum.sem, 1)

            for slot in range(RING):
                pe.sem_inc(unit_done[slot].sem, 1)
            pe.wait_ge(consts_in.sem, 16 * (5 + KD))
            for j in range(KD):
                pe.wait_ge(sq_ready.sem, j + 1)
                for tb in range(TB):
                    mm = pe.matmul(bank[4][:, 8 + tb:9 + tb], sq[:, j % 2, tb * P:(tb + 1) * P], ones[:, 0:1],
                                   start=j == 0 and tb == 0, stop=True, skip_group_check=True)
                mm.then_inc(sq_used.sem, 1)
            for c in range(2):
                if c > 0:
                    pe.wait_ge(mod_ready.sem, c)
                pe.wait_ge(ada_used.sem, 2 + 8 * (c + 1))
                ada_sums()
            pe.wait_ge(diag_ready.sem, 1)
            spread(0, 0, diag[:, :, :].rearrange("p t n -> p (t n)"), 6)

            with pe.Fori(0, DEPTH) as l:
                for f in range(2):
                    u0 = U_FFN[f]

                    def turn(i, ada_on):
                        for pp in range(2):
                            pe.wait_ge(pair_done.sem, pair_done.at(l, f * FT + 2 * i + pp - 1))
                            for part in range(2):
                                slot = unit_ready(pe, l, u0 + 2 * pp + part, i)
                                o = bank[2 * pp + part][:, :]
                                for k in range(KD):
                                    if pp == 0 and part == 0:
                                        pe.wait_ge(h_ready.sem, h_ready.at(l, h_at(2 * f - 1) + k + 1 if f else k + 1 - KD))
                                    mm = product(pe, o, slot, k * P, slice(0, P), hH[:, k], hL[:, k], k == 0,
                                                 k == KD - 1)
                                mm.then_inc(unit_done[slot].sem, 1)
                        if ada_on:
                            c = 7 * f + i
                            pe.wait_ge(mod_ready.sem, mod_ready.at(l, c))
                            pe.wait_ge(ada_used.sem, ada_used.at(l, 8 * (c + 1)))
                            ada_sums()
                    with pe.Fori(0, ADA_FFN[f]) as i:
                        turn(i, True)
                    with pe.Fori(ADA_FFN[f], FT // 2) as i:
                        turn(i, False)
                    n = 2 * f
                    for q in range(FT):
                        a, j = q // (FT // 2), q % (FT // 2)
                        slot = unit_ready(pe, l, u0 + 2 * FT + q)
                        for kt in range(2):
                            k = 2 * j + kt
                            if a == 0:
                                pe.wait_ge(ffn_lo.sem, ffn_lo.at(l, f * FT + k + 1))
                            for mt in range(4):
                                mm = product(pe, bank[4 - 4 * a + mt][:, :], slot, kt * T + mt * P, slice(0, P),
                                             fH[:, k], fL[:, k], k == 0, k == FT - 1)
                        mm.then_inc(unit_done[slot].sem, 1)
                        if FT // 2 < q <= FT // 2 + 4:
                            jj = q - FT // 2 - 1
                            if jj == 0:
                                pe.wait_ge(y_saved.sem, y_saved.at(l, 4 * n + 1))
                            sum_squares(l, sq_at(n, 0) + jj, 0, jj == 0)
                    end_of_boundary(l, n)
                    if f == 0:
                        tensor_mixer(pe, l, sum_squares, spread)
                        end_of_boundary(l, 1)


def _units(w_ffn_in, w_ffn_out):
    gu = w_ffn_in.reshape(KD, P, 2, FT, P).transpose(3, 2, 1, 0, 4).reshape(2 * FT, P, KD * P)
    wo = w_ffn_out.reshape(FT // 2, 2, P, 2, D // 2).transpose(3, 0, 2, 1, 4).reshape(FT, P, KD * P)
    return [gu, wo]


def _tile(w, cols):
    return w[:, cols].reshape(-1, P, len(cols)).transpose(1, 0, 2).reshape(1, P, -1)


def _mixer_units(w_in, w_uq, w_ukv, w_branch, w_out):
    splits = {}
    at = 0
    for name, n in (("a_q", 512), ("a_k", 128), ("a_v", 128), ("i_q", 512), ("i_k", 64), ("i_w", 8), ("r_x", 512),
                    ("r_g", 512), ("c_q", 256), ("c_kv", 160), ("d_q", 512), ("d_k", 128), ("d_v", 128),
                    ("gates", 4096)):
        splits[name] = at
        at += n
    r = np.arange
    swapped = np.r_[ROPE // 2:ROPE, 0:ROPE // 2]
    pairs = lambda o, j: np.r_[o + 64 * j + r(64), o + 64 * (j + 4) + r(64)]

    def cols(name, j):
        s = splits
        if name == "misc":
            kr = s["c_kv"] + P
            return np.r_[np.tile(s["i_w"] + r(8), 8), kr + r(ROPE), kr + swapped]
        if name == "ik":
            return np.tile(s["i_k"] + r(64), 2)
        if name in ("aq", "dq"):
            return pairs(s[name[0] + "_q"], j)
        o = s[{"cq": "c_q", "ckv": "c_kv", "iq": "i_q", "ak": "a_k", "av": "a_v", "dk": "d_k", "dv": "d_v",
               "rx": "r_x", "rg": "r_g"}[name]]
        return o + P * j + r(P)

    branch_at = {n: i for i, n in enumerate("ABCD")}
    out = []
    for it in MIX_UNITS:
        if it[0] == "in":
            out.append(_tile(w_in, cols(it[1], it[2])))
        elif it[0] == "gate":
            out.append(_tile(w_in, splits["gates"] + branch_at[it[1]] * D + P * it[2] + r(P)))
        elif it[0] == "out":
            out.append(_tile(w_out, P * it[1] + r(P)))
        elif it[0] == "branch":
            w = w_branch[branch_at[it[1]]]
            out.append(np.concatenate([_tile(w, P * (2 * it[2] + m) + r(P)) for m in range(2)], axis=2))
        elif it[0] == "uq":
            heads = [96 * (4 * it[1] + i) for i in range(4)]
            out.append(np.concatenate([_tile(w_uq, np.r_[h + r(96), h + 64 + swapped]) for h in heads], axis=2))
        else:
            out.append(_tile(w_ukv, np.r_[np.concatenate([P * h + r(64) for h in range(HEADS)]),
                                          np.concatenate([P * h + 64 + r(64) for h in range(HEADS)])]))
    return out


def _feature_major(a):
    return np.ascontiguousarray(a).reshape(-1, P).T


def _constants():
    q = np.arange(P)[:, None]
    rel = np.arange(T)[None, :] - (T - P)
    dist = (q - rel).astype(np.float32)
    causal = np.where(rel > q, BIG, 0).astype(np.float32)
    rw = np.arange(2 * P)[None, :] - P
    window = np.where((rw <= q) & (q - rw < P), 0, BIG).astype(np.float32)
    half = ROPE // 2
    inv = (np.float32(10000.0) ** (-np.arange(half, dtype=np.float32) / half)).astype(np.float32)
    ang = np.arange(T, dtype=np.float32)[None, :] * inv[:, None]
    cos, sin = np.cos(ang), np.sin(ang)
    rope = np.zeros((P, T), np.float32)
    rope[64:96] = np.concatenate([cos, cos])
    rope[96:128] = np.concatenate([-sin, sin])
    mixc = np.concatenate([dist, causal, (rope * np.float32(-C_SCALE)).astype(np.float32), rope, window], axis=1)
    return np.concatenate([np.eye(P), np.ones((P, P))], axis=1).astype(np.float32), mixc.astype(np.float32)


def kernel(**inputs):
    import concourse.bacc as bacc
    from concourse.bass_utils import run_bass_kernel_spmd

    a = {k: np.asarray(v) for k, v in inputs.items()}
    parts = []
    for l in range(DEPTH):
        parts += _units(a["ffn1_w_in"][l], a["ffn1_w_out"][l])
        parts += _mixer_units(a["w_in"][l], a["mla_w_uq"][l], a["mla_w_ukv"][l], a["w_branch"][l], a["w_out"][l])
        parts += _units(a["ffn2_w_in"][l], a["ffn2_w_out"][l])
    stream = np.concatenate(parts + [parts[0][:RING]], axis=0)

    w_ada = a["w_ada"].reshape(DEPTH, KD, P, NADA, D).transpose(0, 3, 1, 2, 4)
    nxt = [min(l + 1, DEPTH - 1) for l in range(DEPTH)]
    ada = np.concatenate([np.concatenate([w_ada[l, 2:], w_ada[nxt[l], :2]]) for l in range(DEPTH)])
    ada0 = w_ada[0, :2].reshape(2 * KD, P, D)
    pars = []
    for l in range(DEPTH):
        b, bn = _feature_major(a["b_ada"][l]), _feature_major(a["b_ada"][nxt[l]])
        g, gn = _feature_major(a["norm_g"][l]), _feature_major(a["norm_g"][nxt[l]])
        conv = a["conv_w"][l].reshape(4, LRU_T, P).transpose(2, 1, 0).reshape(P, -1)
        pars.append(np.concatenate(
            [b[:, 2 * KD:], bn[:, :2 * KD], gn[:, :KD], g[:, KD:], conv, _feature_major(a["conv_b"][l]),
             _feature_major(a["lru_ba"][l]), _feature_major(a["lru_bx"][l]), _feature_major(a["lru_lambda"][l]),
             _feature_major(a["mla_g_q"][l]), _feature_major(a["mla_g_kv"][l]),
             np.broadcast_to(a["swa_sinks"][l], (P, HEADS))], axis=1))
    pars = np.stack(pars, axis=1)
    par0 = np.concatenate([_feature_major(a["b_ada"][0])[:, :2 * KD], _feature_major(a["norm_g"][0])[:, :KD]], axis=1)
    lruw = np.zeros((DEPTH, P, 2 * LRU_T, P), np.float32)
    for i, name in enumerate(("lru_wa", "lru_wx")):
        for n in range(8):
            rows = slice(64 * (n % 2), 64 * (n % 2) + 64)
            lruw[:, rows, LRU_T * i + n // 2, rows] = a[name][:, n]
    consts, mixc = _constants()
    arrays = {
        "stream": stream, "ada": ada, "ada0": ada0, "pars": pars, "par0": par0, "cvec": _feature_major(a["c"][0]),
        "consts": consts, "mixc": mixc, "lruw": lruw,
        "x_in": a["x"][0].T.reshape(KD, P, T).transpose(1, 0, 2),
    }
    arrays = {k: np.ascontiguousarray(v) for k, v in arrays.items()}
    nc = bacc.Bacc("TRN2", target_bir_lowering=False, num_devices=1)
    args = [nc.dram_tensor(k, v.shape, F32, kind="ExternalInput").ap() for k, v in arrays.items()]
    args.append(nc.dram_tensor("out", (P, KD, T), F32, kind="ExternalOutput").ap())
    trunk_kernel(nc, *args)
    r = run_bass_kernel_spmd(nc, [arrays], core_ids=[0])
    y = r.results[0]["out"]
    return np.ascontiguousarray(y.transpose(1, 0, 2).reshape(D, T).T)[None]
```

```python
from contextlib import ExitStack

import numpy as np

import concourse.bass as bass
from concourse import mybir

F32 = mybir.dt.float32
F32R = mybir.dt.float32r
ALU = mybir.AluOpType
ACT = mybir.ActivationFunctionType
AX_X = mybir.AxisListType.X

P = 128
DEPTH, D, T, FF = 2, 1024, 512, 2816
KD = D // P
TB = T // P
FT = FF // P
HEADS, HD = 8, 64
NOPE, ROPE = 64, 32
TOPK = min(256, T // 4)
NADA = 9
EPS = 1e-6
BIG = 1e30
A_SCALE = HD ** -0.5
C_SCALE = (NOPE + ROPE) ** -0.5
SLOPES = [2.0 ** (-8.0 * i / 16) for i in range(1, 17)]
SLOPE = {"D": SLOPES[:8], "A": SLOPES[8:]}
LRU_T = 512 // P
UNROLL = 4
RING, LEAD = 4, 3

_PAR = [("b_ada", NADA * KD), ("norm_g", 6 * KD), ("conv_w", 4 * LRU_T), ("conv_b", LRU_T), ("ba", LRU_T),
        ("bx", LRU_T), ("lam", LRU_T), ("g_q", 2), ("g_kv", 1), ("sink", HEADS)]
PAR, _at = {}, 0
for _n, _w in _PAR:
    PAR[_n] = _at
    _at += _w
NPAR = _at
ADA_ORDER = [2, 3, 4, 5, 6, 7, 8, 0, 1]
SLOT_OF = {c: i for i, c in enumerate(ADA_ORDER)}



TR_LAG, PV_LAG = 2, 3
END_LAG = HEADS - 1 + PV_LAG
YT_LAG = END_LAG + 1
STEPS = HEADS * TB
STEPS_ALL = STEPS - HEADS + YT_LAG + 1


def mixer_schedule():
    def halves(units):
        for it in units:
            yield ("half", it)
            yield it

    def att(br, fill, topk=()):
        fill, topk = list(halves(fill)), list(topk)
        nf, nt = len(fill), len(topk)
        for st in range(STEPS_ALL):
            yield ("att", br, st)
            while topk and (nt - len(topk)) * STEPS < (st + 1) * nt:
                yield topk.pop(0)
            while fill and (nf - len(fill)) * STEPS_ALL < (st + 1) * nf:
                yield fill.pop(0)

    def merge(n):
        for mp in range(KD // 2):
            yield ("gate", n, 2 * mp)
            yield ("gate", n, 2 * mp + 1)
            yield ("branch", n, mp)

    yield from [("in", "cq", 0), ("in", "cq", 1), ("in", "ckv", 0), ("cstats",), ("in", "misc", 0), ("cbcast",),
                ("in", "iq", 0), ("cnorm",), ("in", "iq", 1), ("uq", 0), ("in", "iq", 2), ("in", "iq", 3), ("uq", 1),
                ("in", "ik", 0), ("krope",), ("ukv",), ("wi",)]
    fill = list(halves([("in", "dk", 0), ("in", "dv", 0)]))
    for n in range(HEADS * (TB - 1)):
        yield ("index", n // HEADS + 1, n % HEADS)
        if n % 6 == 3:
            yield fill.pop(0)
    rounds = [("topk", b, r) for b in range(1, TB) for r in range(TOPK // 8)]
    yield from att("C", [("in", "dq", j) for j in range(4)] + [("in", "aq", j) for j in range(4)] +
                   [("in", "ak", 0), ("in", "av", 0)], rounds[:2 * (TOPK // 8)])
    yield ("vtok", "D")
    yield from att("D", merge("C"), rounds[2 * (TOPK // 8):])
    yield ("vtok", "A")
    yield from att("A", [*merge("D"), *[("in", "rx", j) for j in range(LRU_T)]])
    yield from [("in", "rg", j) for j in range(LRU_T)]
    fill = list(merge("A"))
    for j in range(LRU_T + 1):
        if j < LRU_T:
            yield ("conv", j)
        if j > 0:
            yield ("gelu", j - 1)
        yield fill.pop(0)
        if j < LRU_T:
            yield ("lru", j)
            if j < 3:
                yield fill.pop(0)
    yield ("sqrt",)
    for j in range(LRU_T):
        yield ("scan", j)
        yield fill.pop(0)
    yield from fill
    yield from merge("B")
    yield ("split_merged",)
    for m in range(KD):
        yield ("out", m)


MIXER = list(mixer_schedule())
BRANCHES = ["C", "D", "A", "B"]
Y_OF = {n: i % 2 for i, n in enumerate(BRANCHES)}
ATT = ["C", "D", "A"]
HALVED = {it[1] for it in MIXER if it[0] == "half"}
UNIT_KINDS = ("in", "uq", "ukv", "gate", "branch", "out")
MIX_UNITS = [it for it in MIXER if it[0] in UNIT_KINDS]
U_BANK = {it: c for c, it in enumerate(it for it in MIXER if it[0] in ("in", "gate"))}
V_BANK, _d = {}, 0
for _it in MIXER:
    if _it[0] == "att" and _it[2] >= YT_LAG and (_it[2] - YT_LAG) % HEADS == 0:
        V_BANK[("y", _it[1], (_it[2] - YT_LAG) // HEADS)] = _d
        _d += 1
    if _it[0] == "branch":
        V_BANK[("proj", _it[1], 2 * _it[2])] = _d
        V_BANK[("proj", _it[1], 2 * _it[2] + 1)] = _d + 1
        _d += 2
V_USES = _d

FFN_UNITS = 2 * FT + FT
U_FFN = (0, FFN_UNITS + len(MIX_UNITS))
U_MIX = FFN_UNITS
UNITS = 2 * FFN_UNITS + len(MIX_UNITS)
assert UNITS % RING == 0
U_OF = {it: U_MIX + i for i, it in enumerate(MIX_UNITS)}
ADA_FFN = (5, 3)
ADA_OUT = ADA_FFN[0]
WARM = (10, 16, 1, 11, 6)
ADA_GROUPS = 4
ADA_ROWS = [[[], [0], [1], [2]], [[3], [4], [5, 6], [7]]]
ADA_LOADS = [[[], [0, 1], [2], [3]], [[4], [5], [6], [7]]]


class Signal:

    def __init__(self, sem, per_layer, start=0):
        self.sem, self.per_layer, self.start = sem, per_layer, start

    def at(self, l, n):
        return l * self.per_layer + (self.start + n)


def trunk_kernel(nc, stream, ada, ada0, pars, par0, cvec, consts, mixc, lruw, x_in, out):
    with ExitStack() as ctx:
        base = 16512
        marks = {}

        def at(name, shape, dt, where):
            return nc.alloc_sbuf_tensor_at(name, shape, dt, offset=base + where)

        K = 1024
        x = at("x", [P, KD, T], F32, 0)
        hH = at("h_high", [P, KD, T], F32R, 16 * K)
        hL = at("h_low", [P, KD, T], F32R, 32 * K)
        raw = at("w_raw", [P, RING, 1024], F32, 48 * K)
        wH = at("w_high", [P, RING, 1024], F32R, 64 * K)
        wL = at("w_low", [P, RING, 1024], F32R, 80 * K)
        M0 = 96 * K
        fH = at("ffn_high", [P, FT, T], F32R, M0)
        fL = at("ffn_low", [P, FT, T], F32R, M0 + FT * 2 * K)
        Z0 = M0 + 88 * K
        tanh_g = at("tanh_gate", [P, 2, T], F32, Z0)
        act = at("ffn_act", [P, 2, T], F32, Z0 + 4 * K)
        X0 = Z0 + 8 * K
        ada_raw = at("ada_raw", [P, 2, 1024], F32, X0)
        ada_acc = at("ada_acc", [P, 1024], F32, X0 + 8 * K)
        ada_start = at("ada_start", [P, 2 * KD, 1024], F32, M0)
        sq = at("squares", [P, 2, T], F32, Z0)
        rstd = at("rstd", [P, T], F32, Z0 + 4 * K)
        diag = at("diag", [P, TB, P], F32, Z0 + 6 * K)
        diag2 = at("diag2", [P, 2, TB, P], F32, Z0 + 4 * K)
        y_half = at("y_half", [P, KD // 2, T], F32, X0)
        tu = at("norm_tmp", [P, 2, T], F32, X0 + 8 * K)
        odd_step = at("odd_step", [P, 2, T], F32, M0 + 72 * K)
        yH = [at(f"y_high{i}", [P, 4, T], F32R, M0 + 16 * K * i) for i in range(2)]
        yL = [at(f"y_low{i}", [P, 4, T], F32R, M0 + 16 * K * i + 8 * K) for i in range(2)]
        qC = at("q_mla", [P, HEADS, T], F32, M0 + 16 * K)
        kC = at("k_mla", [P, HEADS, T], F32, M0 + 32 * K)
        vC = at("v_mla", [P, TB, T], F32, X0)
        latent = at("latent", [P, 3, T], F32, M0 + 32 * K)
        merged = at("merged", [P, KD, T], F32, M0 + 32 * K)
        mH = at("merged_high", [P, KD, T], F32R, M0)
        mixcs = at("mixer_consts", [P, 4 * T + 2 * P], F32, M0 + 48 * K)
        dist, causal, rope_q, rope_k = (mixcs[:, i * T:(i + 1) * T] for i in range(4))
        window = mixcs[:, 4 * T:4 * T + 2 * P]
        S0 = M0 + 57 * K
        s_sb = at("scores_sb", [P, 3, T], F32, S0)
        pt_sb = at("probs_t", [P, 2, T], F32, S0 + 6 * K)
        relu_sb = at("relu_dots", [P, 2, T], F32, S0 + 6 * K)
        y_tok = at("y_tok", [P, T], F32, X0 + 8 * K)
        bias_sb = at("bias_sb", [P, T], F32, X0 + 10 * K)
        V0 = M0 + 69 * K
        mL = at("merged_low", [P, KD, T], F32R, V0)
        iq = at("iq", [P, 4, T], F32, V0)
        ik = at("ik", [P, T], F32, V0 + 8 * K)
        pick = {b: at(f"pick{b}", [P, P * (b + 1)], F32, V0 + 10 * K + 64 + 4 * P * [0, 0, 2, 5][b]) for b in range(1, TB)}
        misc = at("misc", [P, T], F32, V0 + 15 * K)
        krope = at("krope", [P, T], F32, V0 + 17 * K)
        aq = at("aq", [P, 4, T], F32, Z0)
        ak = at("ak", [P, T], F32, V0 + 8 * K + 64)
        v_tok = {"D": at("v_tok_d", [P, TB, P], F32, V0 + 15 * K), "A": at("v_tok_a", [P, TB, P], F32, M0 + 52 * K)}
        av = at("av", [P, T], F32, V0 + 17 * K)
        dq = at("dq", [P, 4, T], F32, V0)
        dk = at("dk", [P, T], F32, M0 + 54 * K)
        dv = at("dv", [P, T], F32, M0 + 52 * K)
        gate_t = at("gate_tanh", [P, 2, T], F32, X0)
        gated = at("gated", [P, 2, T], F32, X0 + 4 * K)
        PAD = 3
        rx = at("rx", [P, LRU_T, PAD + T], F32, V0)
        ix = at("gated_x", [P, LRU_T, PAD + T], F32, V0)
        rg = at("rg", [P, LRU_T, T], F32, V0 + 8 * K + 64)
        lru_w = at("lru_w", [P, 2 * LRU_T, P], F32, M0 + 48 * K)
        lru_a = at("lru_a", [P, LRU_T, T], F32, Z0)
        lru_v = at("lru_v", [P, LRU_T, T], F32, S0)
        xc = at("xc", [P, T], F32, S0 + 8 * K)
        ti = at("ti", [P, T], F32, S0 + 10 * K)
        tr = at("tr", [P, T], F32, M0 + 52 * K)
        a_sq = at("a_sq", [P, T], F32, M0 + 54 * K)
        C0 = X0 + 12 * K
        small = {}

        def tiny(name, n):
            small[name] = at(name, [P, n], F32, C0 + marks.setdefault("at", 0))
            marks["at"] += (4 * n + 31) // 32 * 32
            return small[name]

        ident = tiny("ident", P)
        ones = tiny("ones", P)
        parv = tiny("parv", NPAR)
        all_par = at("all_par", [P, DEPTH, NPAR], F32, C0 + marks["at"])
        marks["at"] += (4 * DEPTH * NPAR + 31) // 32 * 32
        mod = tiny("mod", NADA * KD)
        vecA = tiny("vec_scale", KD)
        vecC = tiny("vec_gate", KD)
        cs = tiny("silu_c", KD)
        ms = tiny("mean_sq", 8)
        rs = tiny("rstd_tok", 8)
        mhalf = tiny("minus_half", 8)
        wi = tiny("wi", TB * 8)
        top8 = tiny("top8", 8)
        nmax = tiny("neg_max", 16)
        rsum = tiny("row_sum", 16)
        recip = tiny("recip", 8)
        ctmp = top8
        skt = tiny("sink_tmp", 16)
        nsink = parv[:, PAR["sink"]:PAR["sink"] + HEADS]
        lruv4 = tiny("lru_vectors", 4 * LRU_T)
        hba, hbx, sp4, nsp4 = (lruv4[:, LRU_T * i:LRU_T * (i + 1)] for i in range(4))
        lt = [skt[:, LRU_T * i:LRU_T * (i + 1)] for i in range(4)]
        assert base + C0 + marks["at"] <= nc.sbuf_usable_end, base + C0 + marks["at"] - nc.sbuf_usable_end

        bank = [ctx.enter_context(nc.psum_tensor(f"bank{i}", [P, T], F32)) for i in range(8)]

        def sig(name, per_layer, start=0):
            return Signal(ctx.enter_context(nc.semaphore(name)), per_layer, start)

        per_slot = UNITS // RING
        raw_full = [sig(f"raw_full{i}", 16 * per_slot) for i in range(RING)]
        hi_ready = [sig(f"hi_ready{i}", per_slot) for i in range(RING)]
        lo_ready = [sig(f"lo_ready{i}", per_slot, 1) for i in range(RING)]
        unit_done = [sig(f"unit_done{i}", per_slot, 1) for i in range(RING)]
        consts_in = sig("consts_in", 0)
        x_loaded = sig("x_loaded", 0)
        ada_full = [sig(f"ada_full{i}", 16 * NADA * 4) for i in range(2)]
        ada_used = sig("ada_used", 8 * NADA, 16 + 2)
        ada_start_in = [sig(f"ada_start_in{i}", 0) for i in range(ADA_GROUPS)]
        ada_free = sig("ada_free", 2)
        ada_sum = sig("ada_sum", NADA, 2 + 1)
        mod_ready = sig("mod_ready", NADA, 2)
        c_tanh = sig("c_tanh", 0)
        silu_ready = sig("silu_ready", 0)
        setup_done = sig("setup_done", 0)
        pair_done = sig("pair_done", 2 * FT, 2)
        gate_tanh = sig("ffn_gate_tanh", 2 * FT)
        ffn_hi = sig("ffn_hi", 2 * FT)
        ffn_lo = sig("ffn_lo", 2 * FT, 2)
        NB = 3
        CN = 3
        sq_ready = sig("sq_ready", 2 * KD * NB + CN, KD)
        sq_used = sig("sq_used", 2 * KD * NB + CN, KD + 2)
        y_saved = sig("y_saved", NB * 4)
        ms_ready = sig("ms_ready", 2 * NB + 1, 1)
        rs_ready = sig("rs_ready", 2 * NB + 1, 1)
        diag_ready = sig("diag_ready", 2 * NB + 1, 1)
        bc_ready = sig("bcast_ready", 2 * NB + 1, 1)
        rstd_ready = sig("rstd_ready", NB)
        x_even = sig("x_even", KD // 2 * NB, KD // 2)
        x_odd = sig("x_odd", KD // 2 * NB, KD // 2)
        step_ready = sig("odd_step_ready", KD // 2 * NB)
        u_ready = sig("u_ready", KD * NB + CN, KD)
        hh_ready = sig("h_high_ready", KD * NB + CN, KD)
        h_ready = sig("h_ready", KD * NB + CN, KD)
        mixc_in = sig("mixer_consts_in", 16)
        lru_in = sig("lru_w_in", 16)
        u_evicted = sig("u_evicted", len(U_BANK), 2)
        v_evicted = sig("v_evicted", V_USES, 2)
        qn_evicted = sig("q_nope_evicted", HEADS)
        qr_evicted = sig("q_rope_evicted", HEADS)
        uq_done = sig("uq_done", HEADS - 2)
        kv_done = sig("kv_done", 11)
        kv_evicted = sig("kv_evicted", 12)
        kr_ready = sig("k_rope_ready", 1)
        wi_psum = sig("wi_psum", 1)
        wi_ready = sig("wi_ready", 1)
        NI = HEADS * (TB - 1)
        dots_ready = sig("dots_ready", NI)
        relu_ready = sig("relu_ready", NI)
        index_added = sig("index_added", NI)
        NS = STEPS * len(ATT)
        scores_ready = sig("scores_ready", NS)
        scores_seen = sig("scores_seen", STEPS)
        shifted = sig("shifted", NS)
        probs_ready = sig("probs_ready", NS)
        pt_ready = sig("pt_ready", NS)
        pt_evicted = sig("pt_evicted", NS)
        pv_done = sig("pv_done", NS)
        sink_sum = sig("sink_sum", TB)
        sink_exp = sig("sink_exp", TB)
        ytok_ready = sig("y_tok_ready", TB * len(ATT))
        ytr_ready = sig("y_t_ready", TB * len(ATT))
        yhi_ready = sig("y_high_ready", TB * len(ATT) + LRU_T)
        vt_psum = sig("v_t_psum", 2)
        vt_ready = sig("v_t_ready", 2)
        yb_ready = sig("yb_ready", LRU_T)
        yb_lo = sig("yb_lo", LRU_T)
        conv_ready = sig("conv_ready", LRU_T)
        lru_psum = sig("lru_psum", LRU_T)
        ti_ready = sig("ti_ready", LRU_T)
        asq_ready = sig("a_sq_ready", LRU_T)
        lruv_ready = sig("lru_v_ready", LRU_T)
        rg_sq = sig("rg_sq", LRU_T)
        gelu_in = sig("gelu_in", LRU_T)
        gelu_t = sig("gelu_tanh", LRU_T)
        sqrt_ready = sig("sqrt_ready", 1)
        merged_ready = sig("merged_ready", KD)
        mhi_ready = sig("merged_high", KD)
        mlo_ready = sig("merged_low", KD // 2)
        pads_ready = sig("pads_ready", 1)
        sp_exp = sig("softplus_exp", 1)
        sp_in = sig("softplus_in", 1)
        lru_params = sig("lru_params", 1)
        stored = sig("stored", 0)

        def use_of(l, u):
            if u >= UNITS:
                l, u = l + 1, u - UNITS
            return l, u % RING, u // RING

        def split_high(eng, l, u, i=0):
            l, slot, n = use_of(l, u)
            eng.wait_ge(raw_full[slot].sem, raw_full[slot].at(l, 16 * (n + i + 1)))
            eng.wait_ge(unit_done[slot].sem, unit_done[slot].at(l, n + i))
            eng.activation(wH[:, slot], raw[:, slot], ACT.Copy).then_inc(hi_ready[slot].sem, 1)

        def split_low(eng, l, u, i=0):
            l, slot, n = use_of(l, u)
            eng.wait_ge(hi_ready[slot].sem, hi_ready[slot].at(l, n + i + 1))
            eng.tensor_tensor(wL[:, slot], raw[:, slot], wH[:, slot].bitcast(F32), ALU.subtract
                              ).then_inc(lo_ready[slot].sem, 1)

        def unit_ready(eng, l, u, i=0):
            l, slot, n = use_of(l, u)
            eng.wait_ge(lo_ready[slot].sem, lo_ready[slot].at(l, n + i + 1))
            return slot

        def wait_unit(eng, l, u, i=0):
            l, slot, n = use_of(l, u)
            eng.wait_ge(unit_done[slot].sem, unit_done[slot].at(l, n + i + 1))

        def product(eng, o, slot, col, rows, rhs_h, rhs_l, first, last):
            a, b = wH[rows, slot, col:col + P], wL[rows, slot, col:col + P]
            eng.matmul(o, a, rhs_h, start=first, stop=False)
            eng.matmul(o, a, rhs_l, start=False, stop=False)
            return eng.matmul(o, b, rhs_h, start=False, stop=last)

        def sq_at(n, part):
            return 2 * KD * n + KD * part + (CN if n > 0 else 0)

        def norm_at(n, part):
            return 2 * n + part + (1 if n > 0 else 0)

        def h_at(n):
            return KD * n + (CN if n > 0 else 0)

        block = ctx.enter_context(nc.Block())

        @block.sync
        def _(sp):
            sp.dma_start(parv[:, 0:3 * KD], par0).then_inc(consts_in.sem, 16)
            sp.dma_start(ident[:, :], consts[:, 0:P]).then_inc(consts_in.sem, 16)
            sp.dma_start(ones[:, :], consts[:, P:2 * P]).then_inc(consts_in.sem, 16)
            sp.dma_start(ctmp[:, :], cvec).then_inc(consts_in.sem, 16)
            sp.dma_start(all_par[:, :, :], pars).then_inc(consts_in.sem, 16)
            rows = 2 * KD // ADA_GROUPS
            for g in range(ADA_GROUPS):
                sp.dma_start(ada_start[:, rows * g:rows * (g + 1)], ada0[:, rows * g:rows * (g + 1)]
                             ).then_inc(ada_start_in[g].sem, 16)
                if g == 1:
                    sp.dma_start(x[:, :, :], x_in).then_inc(x_loaded.sem, 16)

            def load_unit(l, u, i=0):
                ll, slot, n = use_of(l, u)
                sp.wait_ge(lo_ready[slot].sem, lo_ready[slot].at(ll, n + i))
                src = stream[bass.ds(l * UNITS + u + RING * i, 1)]
                sp.dma_start(raw[:, slot], src.rearrange("a p n -> p (a n)")).then_inc(raw_full[slot].sem, 16)

            def load_ada(s, src, l, n):
                sp.wait_ge(ada_used.sem, ada_used.at(l, n + s - 1))
                sp.dma_start(ada_raw[:, s % 2], src.rearrange("a b p n -> p (a b n)")).then_inc(
                    ada_full[s % 2].sem, 16)

            for u in range(RING):
                sp.dma_start(raw[:, u], stream[u]).then_inc(raw_full[u].sem, 16)

            with sp.Fori(0, DEPTH) as l:
                for f in range(2):
                    with sp.Fori(0, ADA_FFN[f]) as i:
                        c = i + (ADA_OUT + 1) * f
                        for half in range(2):
                            for j in range(4):
                                load_unit(l, U_FFN[f] + j + RING, 2 * i + half)
                                for s in ADA_LOADS[half][j]:
                                    if s == 0:
                                        sp.wait_ge(ada_free.sem, ada_free.at(l, f + 1))
                                    load_ada(s, ada[bass.ds(l * NADA + c, 1), s:s + 1], l, 8 * c)
                    with sp.Fori(2 * ADA_FFN[f], FT // 2) as i:
                        for j in range(4):
                            load_unit(l, U_FFN[f] + j + RING, i)
                    for v in range(FT):
                        if f == 0 and v < 8:
                            load_ada(v, ada[bass.ds(l * NADA + ADA_OUT, 1), v:v + 1], l, 8 * ADA_OUT)
                        load_unit(l, U_FFN[f] + 2 * FT + v + RING)
                    if f == 0:
                        sp.wait_ge(x_even.sem, x_even.at(l, KD // 2))
                        sp.wait_ge(x_odd.sem, x_odd.at(l, KD // 2))
                        sp.dma_start(mixcs[:, :], mixc).then_inc(mixc_in.sem, 16)
                        for it in MIX_UNITS:
                            load_unit(l, U_OF[it] + RING)
                            if it == ("in", "rg", 0):
                                sp.wait_ge(pv_done.sem, pv_done.at(l, NS))
                                sp.dma_start(lru_w[:, :, :], lruw[bass.ds(l, 1)].rearrange("a p t n -> p (a t) n")
                                             ).then_inc(lru_in.sem, 16)
            for j in range(KD):
                tile = x_odd if j % 2 else x_even
                sp.wait_ge(tile.sem, tile.at(DEPTH - 1, KD + j // 2 + 1))
                sp.dma_start(out[:, j, :], x[:, j, :]).then_inc(stored.sem, 16)
            sp.wait_ge(stored.sem, 16 * KD)
            for slot in range(RING):
                sp.wait_ge(raw_full[slot].sem, raw_full[slot].at(DEPTH, 16))

        @block.gpsimd
        def _(pool):
            pool.memset(mhalf[:, :], -0.5).then_inc(setup_done.sem, 1)
            pool.wait_ge(setup_done.sem, 1)

            def rsqrt(l, n, width):
                pool.wait_ge(ms_ready.sem, ms_ready.at(l, n + 1))
                pool.tensor_tensor(rs[:, 0:width], ms[:, 0:width], mhalf[:, 0:width], ALU.pow
                                   ).then_inc(rs_ready.sem, 1)

            def residual(l, n):
                for i in range(KD // 2):
                    pool.wait_ge(step_ready.sem, step_ready.at(l, n * (KD // 2) + i + 1))
                    pool.tensor_tensor(x[:, 2 * i + 1], x[:, 2 * i + 1], odd_step[:, i % 2], ALU.add
                                       ).then_inc(x_odd.sem, 1)

            with pool.Fori(0, DEPTH) as l:
                rsqrt(l, -1, TB)
                for f in range(2):
                    def turn(i):
                        for pp in range(2):
                            pool.wait_ge(ffn_hi.sem, ffn_hi.at(l, f * FT + 2 * i + pp + 1))
                            m = bass.ds(2 * i + pp, 1)
                            pool.tensor_tensor(fL[:, m, :], act[:, pp:pp + 1, :], fH[:, m, :].bitcast(F32),
                                               ALU.subtract).then_inc(ffn_lo.sem, 1)
                    with pool.Fori(0, FT // 2) as i:
                        turn(i)
                    if f == 0:
                        rsqrt(l, norm_at(0, 0), TB)
                        residual(l, 0)
                        rsqrt(l, norm_at(0, 1), TB)
                        rsqrt(l, 2, 2 * TB)
                        rsqrt(l, norm_at(1, 0), TB)
                        residual(l, 1)
                        rsqrt(l, norm_at(1, 1), TB)
                    else:
                        rsqrt(l, norm_at(2, 0), TB)
                        residual(l, 2)

        def evict(s, l, it, dst, scale=1.0):
            wait_unit(s, l, U_OF[it])
            s.activation(dst, bank[U_BANK[it] % 2][:, :], ACT.Copy, scale=scale).then_inc(u_evicted.sem, 1)

        def merged_high(s, l, m0):
            for m in (m0, m0 + 1):
                s.wait_ge(merged_ready.sem, merged_ready.at(l, m + 1))
                s.activation(mH[:, m], merged[:, m], ACT.Copy).then_inc(mhi_ready.sem, 1)

        def merged_low(v, l, m0):
            for m in (m0, m0 + 1):
                v.wait_ge(mhi_ready.sem, mhi_ready.at(l, m + 1))
                op = v.tensor_tensor(mL[:, m], merged[:, m], mH[:, m].bitcast(F32), ALU.subtract)
            op.then_inc(mlo_ready.sem, 1)

        def att_index(br, st):
            return STEPS * ATT.index(br) + st

        def keys(br, st):
            b, h = st // HEADS, st % HEADS
            k0 = max(0, b - 1) if br == "D" else 0
            return b, h, k0, b + 1 - k0

        def scalar_mixer(s, l, split_high, square, high_parts):
            for it in MIXER:
                kind = it[0]
                if kind in UNIT_KINDS:
                    split_high(s, l, U_OF[it] + LEAD)
                if kind == "in":
                    name, j = it[1], it[2]
                    if name == "cq":
                        evict(s, l, it, latent[:, j])
                    elif name == "ckv":
                        evict(s, l, it, latent[:, 2])
                    elif name == "misc":
                        evict(s, l, it, misc[:, :])
                    elif name == "iq":
                        evict(s, l, it, iq[:, j])
                    elif name == "ik":
                        evict(s, l, it, ik[:, :])
                    elif name == "aq":
                        evict(s, l, it, aq[:, j], -A_SCALE)
                    elif name == "ak":
                        evict(s, l, it, ak[:, :])
                    elif name == "av":
                        evict(s, l, it, av[:, :])
                    elif name == "dq":
                        evict(s, l, it, dq[:, j], -A_SCALE)
                    elif name == "dk":
                        s.wait_ge(qr_evicted.sem, qr_evicted.at(l, HEADS))
                        s.wait_ge(kr_ready.sem, kr_ready.at(l, 1))
                        evict(s, l, it, dk[:, :])
                    elif name == "dv":
                        evict(s, l, it, dv[:, :])
                    elif name == "rx":
                        if j == 0:
                            s.wait_ge(pads_ready.sem, pads_ready.at(l, 1))
                            s.wait_ge(pv_done.sem, pv_done.at(l, 2 * STEPS))
                        evict(s, l, it, rx[:, j, PAD:PAD + T])
                    elif name == "rg":
                        if j == 0:
                            s.wait_ge(pv_done.sem, pv_done.at(l, NS))
                        evict(s, l, it, rg[:, j])
                elif kind == "gate":
                    n, m = it[1], it[2]
                    if n == "C" and m == 0:
                        s.wait_ge(pv_done.sem, pv_done.at(l, STEPS))
                    use = V_BANK.get(("proj", n, m - 2)) if m >= 2 else None
                    if use is None and n != "C":
                        use = V_BANK[("proj", BRANCHES[BRANCHES.index(n) - 1], m + KD - 2)]
                    if use is not None:
                        s.wait_ge(v_evicted.sem, v_evicted.at(l, use + 1))
                    wait_unit(s, l, U_OF[it])
                    s.activation(gate_t[:, m % 2], bank[U_BANK[it] % 2][:, :], ACT.Tanh, scale=0.5
                                 ).then_inc(u_evicted.sem, 1)
                elif kind == "branch" and it[1] == "B" and it[2] > 0:
                    merged_high(s, l, 2 * it[2] - 2)
                elif kind == "cstats":
                    for j in range(CN):
                        if j == 0:
                            s.wait_ge(u_evicted.sem, u_evicted.at(l, U_BANK[("in", "ckv", 0)] + 1))
                        square(l, latent[:, j], sq_at(0, 1) + KD + j)
                elif kind == "cnorm":
                    high_parts(l, h_at(0) + KD, yH[0], CN, None)
                elif kind == "uq":
                    for i in range(4):
                        if i < 3:
                            s.wait_ge(uq_done.sem, uq_done.at(l, 3 * it[1] + i + 1))
                        else:
                            wait_unit(s, l, U_OF[it])
                        s.activation(qC[0:NOPE, 4 * it[1] + i], bank[4 + i][0:NOPE, :], ACT.Copy, scale=-C_SCALE
                                     ).then_inc(qn_evicted.sem, 1)
                elif kind == "ukv":
                    for t in range(12):
                        if t < 11:
                            s.wait_ge(kv_done.sem, kv_done.at(l, t + 1))
                        else:
                            wait_unit(s, l, U_OF[it])
                        src = bank[4 + t % 4]
                        if t < HEADS:
                            s.activation(kC[0:NOPE, t], src[0:NOPE, :], ACT.Copy).then_inc(kv_evicted.sem, 1)
                        else:
                            s.activation(vC[:, t - HEADS], src[:, :], ACT.Copy).then_inc(kv_evicted.sem, 1)
                elif kind == "index":
                    b, h = it[1], it[2]
                    n = HEADS * (b - 1) + h
                    s.wait_ge(dots_ready.sem, dots_ready.at(l, n + 1))
                    if n >= 2:
                        s.wait_ge(index_added.sem, index_added.at(l, n - 1))
                    w = P * (b + 1)
                    s.activation(relu_sb[:, n % 2, 0:w], bank[4 + n % 2][:, 0:w], ACT.Relu
                                 ).then_inc(relu_ready.sem, 1)
                elif kind == "vtok":
                    n = {"D": 0, "A": 1}[it[1]]
                    s.wait_ge(vt_psum.sem, vt_psum.at(l, n + 1))
                    s.activation(v_tok[it[1]][:, :, :], bank[6][:, :].rearrange("p (t n) -> p t n", t=TB), ACT.Copy
                                 ).then_inc(vt_ready.sem, 1)
                elif kind == "att":
                    br, st = it[1], it[2]
                    if TR_LAG <= st < STEPS + TR_LAG:
                        g = att_index(br, st - TR_LAG)
                        b, h, k0, nk = keys(br, st - TR_LAG)
                        s.wait_ge(pt_ready.sem, pt_ready.at(l, g + 1))
                        if g >= 2:
                            s.wait_ge(pv_done.sem, pv_done.at(l, g - 1))
                        s.activation(pt_sb[:, g % 2, 0:P * nk], bank[6][:, 0:P * nk], ACT.Copy
                                     ).then_inc(pt_evicted.sem, 1)
                    blk = (st - (END_LAG - 2)) // HEADS
                    if br == "D" and st >= END_LAG - 2 and (st - (END_LAG - 2)) % HEADS == 0 and blk < TB:
                        s.wait_ge(sink_sum.sem, sink_sum.at(l, blk + 1))
                        s.activation(skt[:, 8:16], skt[:, 0:8], ACT.Exp).then_inc(sink_exp.sem, 1)
                    if st < STEPS:
                        g = att_index(br, st)
                        b, h, k0, nk = keys(br, st)
                        c = 8 * (b % 2) + h
                        s.wait_ge(shifted.sem, shifted.at(l, g + 1))
                        s.activation(s_sb[:, g % 3, 0:P * nk], s_sb[:, g % 3, 0:P * nk], ACT.Exp, scale=-1.0,
                                     bias=nmax[:, c:c + 1], accum_out=rsum[:, c:c + 1]).then_inc(probs_ready.sem, 1)
                    blk = (st - YT_LAG) // HEADS
                    if st >= YT_LAG and (st - YT_LAG) % HEADS == 0:
                        g = TB * ATT.index(br) + blk
                        s.wait_ge(ytr_ready.sem, ytr_ready.at(l, g + 1))
                        use = V_BANK[("y", br, blk)]
                        s.activation(yH[Y_OF[br]][:, :, blk * P:(blk + 1) * P],
                                     bank[2 + use % 2][:, :].rearrange("p (t n) -> p t n", t=4), ACT.Copy
                                     ).then_inc(yhi_ready.sem, 1)
                elif kind == "lru":
                    j = it[1]
                    s.wait_ge(lru_psum.sem, lru_psum.at(l, j + 1))
                    if j >= 1:
                        s.wait_ge(lruv_ready.sem, lruv_ready.at(l, j))
                    s.activation(ti[:, :], bank[5][:, :], ACT.Tanh, scale=0.5, bias=hbx[:, j:j + 1]
                                 ).then_inc(ti_ready.sem, 1)
                    s.activation(tr[:, :], bank[4][:, :], ACT.Tanh, scale=0.5, bias=hba[:, j:j + 1])
                    s.drain()
                    s.activation(lru_a[:, j], tr[:, :], ACT.Exp, scale=nsp4[:, j:j + 1], bias=nsp4[:, j:j + 1])
                    s.drain()
                    s.activation(a_sq[:, :], lru_a[:, j], ACT.Square)
                    s.activation(tr[:, :], tr[:, :], ACT.Tanh, scale=sp4[:, j:j + 1], bias=sp4[:, j:j + 1]
                                 ).then_inc(asq_ready.sem, 1)
                    s.activation(lru_v[:, j], rg[:, j], ACT.Square).then_inc(rg_sq.sem, 1)
                elif kind == "gelu":
                    j = it[1]
                    s.wait_ge(gelu_in.sem, gelu_in.at(l, j + 1))
                    s.activation(lru_v[:, j], lru_v[:, j], ACT.Tanh, scale=0.7978845608028654
                                 ).then_inc(gelu_t.sem, 1)
                elif kind == "sqrt":
                    s.wait_ge(lruv_ready.sem, lruv_ready.at(l, LRU_T))
                    s.activation(lru_v[:, :, :], lru_v[:, :, :], ACT.Sqrt).then_inc(sqrt_ready.sem, 1)
                elif kind == "scan":
                    j = it[1]
                    s.wait_ge(yb_ready.sem, yb_ready.at(l, j + 1))
                    s.activation(yH[Y_OF["B"]][:, j], lru_v[:, j], ACT.Copy).then_inc(yhi_ready.sem, 1)
                elif kind == "split_merged":
                    merged_high(s, l, KD - 2)
                elif kind == "out":
                    m = it[1]
                    if 4 <= m < 8:
                        s.wait_ge(y_saved.sem, y_saved.at(l, 4 + m - 4 + 1))
                        square(l, y_half[:, m - 4], sq_at(1, 0) + m - 4)
                    if m == KD - 1:
                        wait_unit(s, l, U_OF[it])

        @block.scalar
        def _(s):
            def square(l, src, n, extra=None):
                s.wait_ge(sq_used.sem, sq_used.at(l, n if n == -KD else n - 1))
                s.activation(sq[:, n % 2], src, ACT.Square).then_inc(sq_ready.sem, 1)

            def high_parts(l, n, dst, tiles, bias):
                for j in range(tiles):
                    s.wait_ge(u_ready.sem, u_ready.at(l, n + j + 1))
                    if bias is None:
                        s.activation(dst[:, j], tu[:, j % 2], ACT.Copy).then_inc(hh_ready.sem, 1)
                    else:
                        s.activation(dst[:, j], tu[:, j % 2], ACT.Identity, bias=bias(j)).then_inc(hh_ready.sem, 1)

            def shift_col(which):
                c = SLOT_OF[[3, 6, 0][which]]
                return lambda j: mod[:, c * KD + j:c * KD + j + 1]

            def pre_norm(l, n):
                for j in range(KD):
                    tile = x_odd if j % 2 else x_even
                    s.wait_ge(tile.sem, tile.at(l, n * (KD // 2) + j // 2 + 1))
                    square(l, x[:, j], (sq_at(n, 1) if n >= 0 else -KD) + j)
                high_parts(l, h_at(n) if n >= 0 else -KD, hH, KD, shift_col(n % NB))

            def end_of_boundary(l, n):
                for j in range(4, KD):
                    square(l, bank[j - 4][:, :], sq_at(n, 0) + j)
                s.wait_ge(bc_ready.sem, bc_ready.at(l, norm_at(n, 0) + 1))
                s.activation(rstd[:, :], bank[5][:, :], ACT.Copy).then_inc(rstd_ready.sem, 1)
                if n < NB - 1:
                    pre_norm(l, n)

            s.wait_ge(consts_in.sem, 16 * 5)
            s.activation(mod[:, 0:KD], ctmp[:, :], ACT.Tanh, scale=0.5).then_inc(c_tanh.sem, 1)
            for u in range(LEAD):
                s.wait_ge(raw_full[u].sem, 16)
                s.wait_ge(unit_done[u].sem, 1)
                s.activation(wH[:, u], raw[:, u], ACT.Copy).then_inc(hi_ready[u].sem, 1)

            s.wait_ge(x_loaded.sem, 16)
            with s.Fori(0, DEPTH) as l:
                pre_norm(l, -1)
                for f in range(2):
                    u0 = U_FFN[f]

                    def turn(i):
                        for pp in range(2):
                            m = f * FT + 2 * i + pp
                            split_high(s, l, u0 + 2 * pp + LEAD, i)
                            wait_unit(s, l, u0 + 2 * pp, i)
                            s.wait_ge(pair_done.sem, pair_done.at(l, m - 1))
                            s.activation(tanh_g[:, pp], bank[2 * pp][:, :], ACT.Tanh, scale=0.5
                                         ).then_inc(gate_tanh.sem, 1)
                            split_high(s, l, u0 + 2 * pp + 1 + LEAD, i)
                            s.wait_ge(pair_done.sem, pair_done.at(l, m + 1))
                            s.activation(fH[:, bass.ds(2 * i + pp, 1), :], act[:, pp:pp + 1, :], ACT.Copy
                                         ).then_inc(ffn_hi.sem, 1)
                    with s.Fori(0, FT // 2) as i:
                        turn(i)
                    if f == 0:
                        s.wait_ge(sp_in.sem, sp_in.at(l, 1))
                        s.activation(lt[1][:, :], lt[0][:, :], ACT.Exp, scale=-1.0).then_inc(sp_exp.sem, 1)
                    n = 2 * f
                    for v in range(FT):
                        split_high(s, l, u0 + 2 * FT + v + LEAD)
                        if FT // 2 < v <= FT // 2 + 4:
                            j = v - FT // 2 - 1
                            s.wait_ge(y_saved.sem, y_saved.at(l, 4 * n + j + 1))
                            square(l, y_half[:, j], sq_at(n, 0) + j)
                    wait_unit(s, l, u0 + FFN_UNITS - 1)
                    end_of_boundary(l, n)
                    if f == 0:
                        scalar_mixer(s, l, split_high, square, high_parts)
                        end_of_boundary(l, 1)

        def pars_load(v, l):
            v.tensor_copy(parv[:, :], all_par[:, bass.ds(l, 1), :].rearrange("p a n -> p (a n)"))
            v.drain()

        def lru_parameters(v, l):
            lam = parv[:, PAR["lam"]:PAR["lam"] + LRU_T]
            v.scalar_tensor_tensor(lt[0][:, :], lam, -1.0, lam, ALU.mult, ALU.max).then_inc(sp_in.sem, 1)
            v.tensor_scalar(hba[:, :], parv[:, PAR["ba"]:PAR["ba"] + LRU_T], 0.5, None, ALU.mult)
            v.tensor_scalar(hbx[:, :], parv[:, PAR["bx"]:PAR["bx"] + LRU_T], 0.5, None, ALU.mult)
            v.tensor_scalar(nsink, nsink, -1.0, None, ALU.mult)
            v.wait_ge(sp_exp.sem, sp_exp.at(l, 1))
            v.tensor_scalar(lt[2][:, :], lt[1][:, :], 2.0, None, ALU.add)
            v.drain()
            v.reciprocal(lt[3][:, :], lt[2][:, :])
            v.drain()
            v.tensor_tensor(lt[1][:, :], lt[1][:, :], lt[3][:, :], ALU.mult)
            v.drain()
            v.tensor_tensor(lt[2][:, :], lt[1][:, :], lt[1][:, :], ALU.mult)
            v.drain()
            v.tensor_scalar(lt[3][:, :], lt[2][:, :], 1.0 / 19, 1.0 / 17, ALU.mult, ALU.add)
            for k in (15, 13, 11, 9, 7, 5, 3, 1):
                v.drain()
                v.tensor_tensor(lt[3][:, :], lt[3][:, :], lt[2][:, :], ALU.mult)
                v.drain()
                v.tensor_scalar(lt[3][:, :], lt[3][:, :], 1.0 / k, None, ALU.add)
            v.drain()
            v.tensor_tensor(lt[3][:, :], lt[3][:, :], lt[1][:, :], ALU.mult)
            v.tensor_scalar(lt[2][:, :], lam, -1.0, 0.0, ALU.mult, ALU.max)
            v.drain()
            v.scalar_tensor_tensor(lt[3][:, :], lt[3][:, :], 2.0, lt[2][:, :], ALU.mult, ALU.add)
            v.drain()
            v.tensor_scalar(sp4[:, :], lt[3][:, :], 4.0, None, ALU.mult)
            v.tensor_scalar(nsp4[:, :], lt[3][:, :], -4.0, None, ALU.mult).then_inc(lru_params.sem, 1)

        def vector_mixer(v, l, diagonal, normalise, save_half):
            for it in MIXER:
                kind = it[0]
                if kind in UNIT_KINDS:
                    split_low(v, l, U_OF[it] + LEAD)
                v.drain()
                if kind == "in" and it[1] == "rx" and it[2] == 0:
                    v.wait_ge(pv_done.sem, pv_done.at(l, 2 * STEPS))
                    v.memset(rx[:, :, 0:PAD], 0.0).then_inc(pads_ready.sem, 1)
                elif kind == "cstats":
                    v.wait_ge(sq_used.sem, sq_used.at(l, 2 * KD + CN))
                    v.tensor_scalar(ms[:, 0:TB], bank[7][:, 0:TB], 1.0 / 256, EPS, ALU.mult, ALU.add)
                    v.drain()
                    v.tensor_scalar(ms[:, TB:2 * TB], bank[7][:, 8:8 + TB], 1.0 / P, EPS, ALU.mult, ALU.add
                                    ).then_inc(ms_ready.sem, 1)
                elif kind == "cbcast":
                    v.wait_ge(rs_ready.sem, rs_ready.at(l, 3))
                    diagonal(l, 2, diag2[:, 0], 0)
                    v.drain()
                    diagonal(l, 2, diag2[:, 1], TB).then_inc(diag_ready.sem, 1)
                elif kind == "cnorm":
                    v.wait_ge(bc_ready.sem, bc_ready.at(l, 3))
                    g = PAR["g_q"]
                    normalise(l, h_at(0) + KD, lambda j: latent[:, j], lambda j: parv[:, g + j:g + j + 1],
                              lambda j: bank[5 + j // 2][:, :], yH[0], yL[0], CN, None)
                elif kind == "uq":
                    v.wait_ge(mixc_in.sem, mixc_in.at(l, 16))
                    for i in range(4):
                        h = 4 * it[1] + i
                        if i < 3:
                            v.wait_ge(uq_done.sem, uq_done.at(l, 3 * it[1] + i + 1))
                        else:
                            wait_unit(v, l, U_OF[it])
                        v.tensor_tensor(krope[64:96, :], bank[4 + i][96:128, :], rope_q[96:128, :], ALU.mult)
                        v.tensor_tensor(qC[64:96, h], bank[4 + i][64:96, :], rope_q[64:96, :], ALU.mult)
                        v.drain()
                        v.tensor_tensor(qC[64:96, h], qC[64:96, h], krope[64:96, :], ALU.add
                                        ).then_inc(qr_evicted.sem, 1)
                        v.drain()
                elif kind == "krope":
                    v.drain()
                    v.wait_ge(u_evicted.sem, u_evicted.at(l, U_BANK[("in", "misc", 0)] + 1))
                    v.tensor_tensor(kC[64:96, 0], misc[64:96, :], rope_k[64:96, :], ALU.mult)
                    v.tensor_tensor(kC[64:96, 1], misc[96:128, :], rope_k[96:128, :], ALU.mult)
                    v.drain()
                    v.tensor_tensor(kC[64:96, 2], kC[64:96, 0], kC[64:96, 1], ALU.add)
                    v.drain()
                    v.tensor_copy(kC[64:96, 0:2, :], kC[64:96, 2:3, :].broadcast_to([32, 2, T]))
                    v.tensor_copy(kC[64:96, 3:HEADS, :], kC[64:96, 2:3, :].broadcast_to([32, HEADS - 3, T])
                                  ).then_inc(kr_ready.sem, 1)
                elif kind == "wi":
                    v.wait_ge(wi_psum.sem, wi_psum.at(l, 1))
                    v.tensor_copy(wi[:, :].rearrange("p (t h) -> p t h", t=TB),
                                  bank[6][:, :].rearrange("p (t n) -> p t n", t=TB)[:, :, 0:8]).then_inc(wi_ready.sem, 1)
                    v.drain()
                elif kind == "index":
                    b, h = it[1], it[2]
                    n = HEADS * (b - 1) + h
                    w = P * (b + 1)
                    c = 8 * b + h
                    if h > 0:
                        v.drain()
                    v.wait_ge(relu_ready.sem, relu_ready.at(l, n + 1))
                    if h == 0:
                        v.tensor_scalar(pick[b][:, :], relu_sb[:, n % 2, 0:w], wi[:, c:c + 1], None, ALU.mult
                                        ).then_inc(index_added.sem, 1)
                    else:
                        v.scalar_tensor_tensor(pick[b][:, :], relu_sb[:, n % 2, 0:w], wi[:, c:c + 1], pick[b][:, :],
                                               ALU.mult, ALU.add).then_inc(index_added.sem, 1)
                    if h == HEADS - 1:
                        v.drain()
                        v.scalar_tensor_tensor(pick[b][:, w - P:w], causal[:, T - P:T], -1e8, pick[b][:, w - P:w],
                                               ALU.mult, ALU.add)
                elif kind == "topk":
                    b, r = it[1], it[2]
                    v.drain()
                    v.max(top8[:, :], pick[b][:, :])
                    v.drain()
                    v.match_replace(pick[b][:, :], top8[:, :], pick[b][:, :], -3e38)
                    if r == TOPK // 8 - 1:
                        v.drain()
                        v.tensor_scalar(pick[b][:, :], pick[b][:, :], -2e38, BIG, ALU.is_gt, ALU.mult)
                elif kind == "att":
                    vector_attention(v, l, it[1], it[2])
                elif kind == "branch":
                    n, mp = it[1], it[2]
                    wait_unit(v, l, U_OF[it])
                    for m in (2 * mp, 2 * mp + 1):
                        gate = gate_t[:, m % 2]
                        v.wait_ge(u_evicted.sem, u_evicted.at(l, U_BANK[("gate", n, m)] + 1))
                        src = bank[2 + V_BANK[("proj", n, m)] % 2][:, :]
                        if n == BRANCHES[0]:
                            v.scalar_tensor_tensor(merged[:, m], gate, 1.0, src, ALU.add, ALU.mult
                                                   ).then_inc(v_evicted.sem, 1)
                        else:
                            v.scalar_tensor_tensor(gated[:, m % 2], gate, 1.0, src, ALU.add, ALU.mult
                                                   ).then_inc(v_evicted.sem, 1)
                            v.drain()
                            op = v.tensor_tensor(merged[:, m], merged[:, m], gated[:, m % 2], ALU.add)
                            if n == BRANCHES[-1]:
                                op.then_inc(merged_ready.sem, 1)
                    if n == BRANCHES[-1] and mp > 0:
                        merged_low(v, l, 2 * mp - 2)
                elif kind == "conv":
                    j = it[1]
                    w0 = PAR["conv_w"] + 4 * j
                    v.drain()
                    if j == 0:
                        v.wait_ge(u_evicted.sem, u_evicted.at(l, U_BANK[("in", "rg", LRU_T - 1)] + 1))
                    v.tensor_scalar(xc[:, :], rx[:, j, 0:T], parv[:, w0:w0 + 1],
                                    parv[:, PAR["conv_b"] + j:PAR["conv_b"] + j + 1], ALU.mult, ALU.add)
                    for k in range(1, 4):
                        v.drain()
                        op = v.scalar_tensor_tensor(xc[:, :], rx[:, j, k:k + T], parv[:, w0 + k:w0 + k + 1],
                                                    xc[:, :], ALU.mult, ALU.add)
                    op.then_inc(conv_ready.sem, 1)
                elif kind == "lru":
                    j = it[1]
                    v.drain()
                    v.wait_ge(ti_ready.sem, ti_ready.at(l, j + 1))
                    v.scalar_tensor_tensor(ix[:, j, 0:T], ti[:, :], 1.0, xc[:, :], ALU.add, ALU.mult)
                    v.wait_ge(rg_sq.sem, rg_sq.at(l, j + 1))
                    v.tensor_scalar(lru_v[:, j], lru_v[:, j], 0.044715, 1.0, ALU.mult, ALU.add)
                    v.drain()
                    v.tensor_tensor(lru_v[:, j], lru_v[:, j], rg[:, j], ALU.mult).then_inc(gelu_in.sem, 1)
                elif kind == "gelu":
                    j = it[1]
                    v.wait_ge(gelu_t.sem, gelu_t.at(l, j + 1))
                    v.scalar_tensor_tensor(rg[:, j], lru_v[:, j], 1.0, rg[:, j], ALU.add, ALU.mult)
                    v.drain()
                    v.wait_ge(asq_ready.sem, asq_ready.at(l, j + 1))
                    v.scalar_tensor_tensor(lru_v[:, j], a_sq[:, :], 1.0, tr[:, :], ALU.add, ALU.mult
                                           ).then_inc(lruv_ready.sem, 1)
                elif kind == "scan":
                    j = it[1]
                    v.drain()
                    if j == 0:
                        v.wait_ge(sqrt_ready.sem, sqrt_ready.at(l, 1))
                    v.tensor_tensor(ix[:, j, 0:T], ix[:, j, 0:T], lru_v[:, j], ALU.mult)
                    v.drain()
                    v.tensor_tensor_scan(lru_v[:, j], lru_a[:, j], ix[:, j, 0:T], 0.0, ALU.mult, ALU.add)
                    v.drain()
                    v.scalar_tensor_tensor(lru_v[:, j], lru_v[:, j], 0.25, rg[:, j], ALU.mult, ALU.mult
                                           ).then_inc(yb_ready.sem, 1)
                    v.drain()
                    v.wait_ge(yhi_ready.sem, yhi_ready.at(l, TB * len(ATT) + j + 1))
                    v.tensor_tensor(yL[Y_OF["B"]][:, j], lru_v[:, j], yH[Y_OF["B"]][:, j].bitcast(F32), ALU.subtract
                                    ).then_inc(yb_lo.sem, 1)
                elif kind == "split_merged":
                    merged_low(v, l, KD - 2)
                elif kind == "out" and it[1] >= 4:
                    if it[1] == 4:
                        v.drain()
                        wait_unit(v, l, U_OF[("out", 3)])
                    save_half(l, 1, it[1] - 4)

        def vector_attention(v, l, br, st):
            blk = (st - (END_LAG - 2)) // HEADS
            if br == "D" and st >= END_LAG - 2 and (st - (END_LAG - 2)) % HEADS == 0 and blk < TB:
                cols = slice(8 * (blk % 2), 8 * (blk % 2) + 8)
                v.drain()
                v.tensor_tensor(skt[:, 0:8], nmax[:, cols], nsink, ALU.subtract).then_inc(sink_sum.sem, 1)
            blk = (st - (END_LAG - 1)) // HEADS
            if st >= END_LAG - 1 and (st - (END_LAG - 1)) % HEADS == 0 and blk < TB:
                cols = slice(8 * (blk % 2), 8 * (blk % 2) + 8)
                v.wait_ge(probs_ready.sem, probs_ready.at(l, att_index(br, HEADS * blk + HEADS - 1) + 1))
                if br == "D":
                    v.wait_ge(sink_exp.sem, sink_exp.at(l, blk + 1))
                    v.tensor_tensor(rsum[:, cols], rsum[:, cols], skt[:, 8:16], ALU.add)
                    v.drain()
                v.reciprocal(recip[:, :], rsum[:, cols])
            if st < STEPS:
                g = att_index(br, st)
                b, h, k0, nk = keys(br, st)
                w = P * nk
                if br == "C":
                    bias = causal[:, T - w:T]
                else:
                    if br == "D":
                        mask = window[:, 2 * P - w:2 * P]
                    else:
                        mask = causal[:, T - P:T] if b == 0 else pick[b][:, :]
                    bias = bias_sb[:, 0:w]
                v.drain()
                if g >= 3:
                    v.wait_ge(pt_ready.sem, pt_ready.at(l, g - 2))
                v.wait_ge(scores_ready.sem, scores_ready.at(l, g + 1))
                if br == "C":
                    v.sem_inc(scores_seen.sem, 1)
                else:
                    v.scalar_tensor_tensor(bias, dist[:, T - w:T], SLOPE[br][h], mask, ALU.mult, ALU.add)
                    v.drain()
                c = 8 * (b % 2) + h
                first = nsink[:, h:h + 1] if br == "D" else 3e38
                v.tensor_tensor_reduce(s_sb[:, g % 3, 0:w], bank[4 + g % 2][:, 0:w], bias, 1.0, first, ALU.add,
                                       ALU.min, nmax[:, c:c + 1]).then_inc(shifted.sem, 1)
            blk = (st - END_LAG) // HEADS
            if st >= END_LAG and (st - END_LAG) % HEADS == 0 and blk < TB:
                g = TB * ATT.index(br) + blk
                v.drain()
                if g >= 1:
                    v.wait_ge(ytr_ready.sem, ytr_ready.at(l, g))
                v.wait_ge(pv_done.sem, pv_done.at(l, att_index(br, HEADS * blk + HEADS - 1) + 1))
                v.tensor_tensor(y_tok[:, :].rearrange("p (h d) -> p h d", h=HEADS),
                                bank[7][:, :].rearrange("p (h d) -> p h d", h=HEADS),
                                recip[:, :, None].broadcast_to([P, HEADS, HD]), ALU.mult).then_inc(ytok_ready.sem, 1)
            blk = (st - YT_LAG) // HEADS
            if st >= YT_LAG and (st - YT_LAG) % HEADS == 0:
                g = TB * ATT.index(br) + blk
                v.wait_ge(yhi_ready.sem, yhi_ready.at(l, g + 1))
                cols = slice(blk * P, (blk + 1) * P)
                use = V_BANK[("y", br, blk)]
                i = Y_OF[br]
                v.tensor_tensor(yL[i][:, :, cols], bank[2 + use % 2][:, :].rearrange("p (t n) -> p t n", t=4),
                                yH[i][:, :, cols].bitcast(F32), ALU.subtract).then_inc(v_evicted.sem, 1)

        @block.vector
        def _(v):
            def mean_square(eps):
                for tb in range(TB):
                    cols = slice(tb * P, (tb + 1) * P)
                    op = v.tensor_tensor_reduce(diag[:, tb, :], bank[4][:, cols], ident[:, :], 1.0 / D, eps, ALU.mult,
                                                ALU.add, ms[:, tb:tb + 1])
                return op

            def diagonal(l, n, dst, col):
                return v.tensor_tensor(dst, ident[:, None, :].broadcast_to([P, TB, P]),
                                       rs[:, col:col + TB][:, :, None].broadcast_to([P, TB, P]), ALU.mult)

            def normalise(l, n, src, scale, bc, dst_h, dst_l, tiles, bias):
                def low(j):
                    v.wait_ge(hh_ready.sem, hh_ready.at(l, n + j + 1))
                    if bias is None:
                        v.tensor_tensor(dst_l[:, j], tu[:, j % 2], dst_h[:, j].bitcast(F32), ALU.subtract
                                        ).then_inc(h_ready.sem, 1)
                    else:
                        v.scalar_tensor_tensor(dst_l[:, j], tu[:, j % 2], bias(j), dst_h[:, j].bitcast(F32),
                                               ALU.add, ALU.subtract).then_inc(h_ready.sem, 1)
                for j in range(tiles):
                    if j >= 2:
                        v.drain()
                    v.scalar_tensor_tensor(tu[:, j % 2], src(j), scale(j), bc(j), ALU.mult, ALU.mult
                                           ).then_inc(u_ready.sem, 1)
                    if j >= 1:
                        low(j - 1)
                low(tiles - 1)
                v.drain()

            def shift_col(which):
                c = SLOT_OF[[3, 6, 0][which]]
                return lambda j: mod[:, c * KD + j:c * KD + j + 1]

            def pre_vector(which):
                c = SLOT_OF[[4, 7, 1][which]] * KD
                g = PAR["norm_g"] + [2, 4, 0][which] * KD
                v.scalar_tensor_tensor(vecA[:, :], mod[:, c:c + KD], 1.0, parv[:, g:g + KD], ALU.add, ALU.mult)

            def vectors(which):
                c = SLOT_OF[[2, 5, 8][which]] * KD
                g = PAR["norm_g"] + [1, 3, 5][which] * KD
                v.scalar_tensor_tensor(vecC[:, :], mod[:, c:c + KD], [0.5, 1.0, 0.5][which], parv[:, g:g + KD],
                                       ALU.mult, ALU.mult)
                pre_vector(which)

            def save_half(l, n, j):
                v.tensor_copy(y_half[:, j], bank[4 + j][:, :]).then_inc(y_saved.sem, 1)

            def end_of_boundary(l, n):
                v.drain()
                vectors(n)
                v.drain()
                v.wait_ge(sq_used.sem, sq_used.at(l, sq_at(n, 0) + KD))
                mean_square(4 * EPS).then_inc(ms_ready.sem, 1)
                v.wait_ge(rs_ready.sem, rs_ready.at(l, norm_at(n, 0) + 1))
                diagonal(l, n, diag[:, :, :], 0).then_inc(diag_ready.sem, 1)
                v.wait_ge(rstd_ready.sem, rstd_ready.at(l, n + 1))
                for i in range(KD // 2):
                    if i >= 2:
                        v.wait_ge(x_odd.sem, x_odd.at(l, n * (KD // 2) + i - 1))
                    for j, dst in ((2 * i + 1, odd_step), (2 * i, tu)):
                        y = y_half[:, j] if j < 4 else bank[j - 4][:, :]
                        op = v.scalar_tensor_tensor(dst[:, i % 2], y, vecC[:, j:j + 1], rstd[:, :], ALU.mult, ALU.mult)
                        if j % 2:
                            op.then_inc(step_ready.sem, 1)
                    v.drain()
                    v.tensor_tensor(x[:, 2 * i], x[:, 2 * i], tu[:, i % 2], ALU.add).then_inc(x_even.sem, 1)
                v.drain()
                if n < NB - 1:
                    pre_norm(l, n)

            def pre_norm(l, n):
                nth = norm_at(n, 1) if n >= 0 else -1
                v.wait_ge(sq_used.sem, sq_used.at(l, (sq_at(n, 1) if n >= 0 else -KD) + KD))
                mean_square(EPS).then_inc(ms_ready.sem, 1)
                v.wait_ge(rs_ready.sem, rs_ready.at(l, nth + 1))
                diagonal(l, n, diag[:, :, :], 0).then_inc(diag_ready.sem, 1)
                v.wait_ge(bc_ready.sem, bc_ready.at(l, nth + 1))
                normalise(l, h_at(n) if n >= 0 else -KD, lambda j: x[:, j], lambda j: vecA[:, j:j + 1],
                          lambda j: bank[6][:, :], hH, hL, KD, shift_col(n % NB))

            def ada_step(s, src=None):
                src = ada_raw[:, s % 2] if src is None else src
                if s == 0:
                    v.tensor_scalar(ada_acc[:, :], src, cs[:, 0:1], None, ALU.mult
                                    ).then_inc(ada_used.sem, 1)
                else:
                    v.scalar_tensor_tensor(ada_acc[:, :], src, cs[:, s:s + 1], ada_acc[:, :],
                                           ALU.mult, ALU.add).then_inc(ada_used.sem, 1)

            for slot in range(RING):
                v.sem_inc(lo_ready[slot].sem, 1)
            v.sem_inc(ada_used.sem, 2)
            v.sem_inc(x_even.sem, KD // 2)
            v.sem_inc(x_odd.sem, KD // 2)
            v.sem_inc(ada_sum.sem, 1)
            v.sem_inc(pair_done.sem, 2)
            v.sem_inc(ffn_lo.sem, 2)
            v.sem_inc(u_evicted.sem, 2)
            v.sem_inc(v_evicted.sem, 2)
            v.wait_ge(c_tanh.sem, 1)
            v.scalar_tensor_tensor(cs[:, :], mod[:, 0:KD], 1.0, ctmp[:, :], ALU.add, ALU.mult)
            v.drain()
            v.tensor_scalar(cs[:, :], cs[:, :], 0.5, None, ALU.mult)
            for c in range(2):
                v.drain()
                v.wait_ge(ada_sum.sem, c + 1)
                for s in range(8):
                    if s > 0:
                        v.drain()
                    v.wait_ge(ada_start_in[(8 * c + s) * ADA_GROUPS // 16].sem, 16)
                    ada_step(s, ada_start[:, 8 * c + s])
                v.wait_ge(ada_sum.sem, c + 2)
                v.tensor_tensor(mod[:, (7 + c) * KD:(8 + c) * KD], bank[7][:, 0:KD], parv[:, c * KD:(c + 1) * KD],
                                ALU.add).then_inc(mod_ready.sem, 1)
            v.drain()
            v.scalar_tensor_tensor(vecA[:, :], mod[:, 8 * KD:9 * KD], 1.0, parv[:, 2 * KD:3 * KD], ALU.add, ALU.mult)
            for u in range(LEAD):
                v.wait_ge(hi_ready[u].sem, 1)
                v.tensor_tensor(wL[:, u], raw[:, u], wH[:, u].bitcast(F32), ALU.subtract
                                ).then_inc(lo_ready[u].sem, 1)
            with v.Fori(0, DEPTH) as l:
                v.drain()
                pars_load(v, l)
                pre_norm(l, -1)
                v.sem_inc(ada_free.sem, 1)
                for f in range(2):
                    u0 = U_FFN[f]

                    c0 = (ADA_OUT + 1) * f

                    def add_bias(c):
                        v.wait_ge(ada_sum.sem, ada_sum.at(l, c + 1))
                        v.tensor_tensor(mod[:, bass.ds(c * KD, KD)], bank[7][:, 0:KD],
                                        parv[:, bass.ds(PAR["b_ada"] + c * KD, KD)], ALU.add
                                        ).then_inc(mod_ready.sem, 1)

                    def turn(i, half=0, c=None, before=None):
                        def steps(group):
                            if c is not None:
                                if 0 in ADA_ROWS[half][group]:
                                    if before is not None:
                                        add_bias(before)
                                    v.wait_ge(ada_sum.sem, ada_sum.at(l, c))
                                for s in ADA_ROWS[half][group]:
                                    if s > 0:
                                        v.drain()
                                    full = ada_full[s % 2]
                                    v.wait_ge(full.sem, full.at(l, 16 * (4 * c + s // 2 + 1)))
                                    ada_step(s)
                        for pp in range(2):
                            m = f * FT + 2 * i + pp
                            split_low(v, l, u0 + 2 * pp + LEAD, i)
                            steps(2 * pp)
                            v.wait_ge(ffn_lo.sem, ffn_lo.at(l, m - 1))
                            v.wait_ge(gate_tanh.sem, gate_tanh.at(l, m + 1))
                            v.scalar_tensor_tensor(act[:, pp], tanh_g[:, pp], 1.0, bank[2 * pp][:, :], ALU.add,
                                                   ALU.mult)
                            split_low(v, l, u0 + 2 * pp + 1 + LEAD, i)
                            steps(2 * pp + 1)
                            v.drain()
                            wait_unit(v, l, u0 + 2 * pp + 1, i)
                            v.tensor_tensor(act[:, pp], act[:, pp], bank[2 * pp + 1][:, :], ALU.mult
                                            ).then_inc(pair_done.sem, 1)
                    turn(0, 0, c0)
                    turn(1, 1, c0)
                    with v.Fori(1, ADA_FFN[f]) as i:
                        turn(2 * i, 0, i + c0, i + (c0 - 1))
                        turn(2 * i + 1, 1, i + c0)
                    add_bias(c0 + ADA_FFN[f] - 1)
                    with v.Fori(2 * ADA_FFN[f], FT // 2) as i:
                        turn(i)
                    if f == 0:
                        lru_parameters(v, l)
                    n = 2 * f
                    for q in range(FT):
                        split_low(v, l, u0 + 2 * FT + q + LEAD)
                        if f == 0 and q < 8:
                            if q == 0:
                                v.wait_ge(ada_sum.sem, ada_sum.at(l, ADA_OUT))
                            else:
                                v.drain()
                            v.wait_ge(ada_full[q % 2].sem, ada_full[q % 2].at(l, 16 * (4 * ADA_OUT + q // 2 + 1)))
                            ada_step(q)
                        if f == 0 and q == 9:
                            v.wait_ge(ada_sum.sem, ada_sum.at(l, ADA_OUT + 1))
                            b0 = PAR["b_ada"] + ADA_OUT * KD
                            v.tensor_tensor(mod[:, ADA_OUT * KD:(ADA_OUT + 1) * KD], bank[0][:, 0:KD],
                                            parv[:, b0:b0 + KD], ALU.add).then_inc(mod_ready.sem, 1)
                        if FT // 2 < q <= FT // 2 + 4:
                            j = q - FT // 2 - 1
                            if j == 0:
                                wait_unit(v, l, u0 + 2 * FT + FT // 2 - 1)
                            save_half(l, n, j)
                    end_of_boundary(l, n)
                    if f == 0:
                        vector_mixer(v, l, diagonal, normalise, save_half)
                        end_of_boundary(l, 1)
                        v.sem_inc(ada_free.sem, 1)
            v.drain()

        def tensor_mixer(pe, l, sum_squares, spread):
            slots = [unit_ready(pe, l, U_OF[it]) for it in MIXER[:2]]
            pe.wait_ge(u_evicted.sem, u_evicted.at(l, 0))
            for k in range(KD):
                pe.wait_ge(h_ready.sem, h_ready.at(l, h_at(0) + k + 1))
                for j, slot in enumerate(slots):
                    mm = product(pe, bank[j][:, :], slot, k * P, slice(0, P), hH[:, k], hL[:, k], k == 0, k == KD - 1)
                    if k == KD - 1:
                        mm.then_inc(unit_done[slot].sem, 1)
            for it in MIXER[2:]:
                first, last = (True, False) if it[0] == "half" else (it not in HALVED, True)
                if it[0] == "half":
                    it = it[1]
                kind = it[0]
                if kind in ("in", "gate"):
                    slot = U_OF[it] % RING
                    c = U_BANK[it]
                    if first:
                        unit_ready(pe, l, U_OF[it])
                        pe.wait_ge(u_evicted.sem, u_evicted.at(l, c - 1))
                    for k in range(0 if first else KD // 2, KD if last else KD // 2):
                        mm = product(pe, bank[c % 2][:, :], slot, k * P, slice(0, P), hH[:, k], hL[:, k], k == 0,
                                     k == KD - 1)
                    if last:
                        mm.then_inc(unit_done[slot].sem, 1)
                elif kind == "cstats":
                    n0 = sq_at(0, 1) + KD
                    for j in range(CN):
                        col = 8 if j == 2 else 0
                        pe.wait_ge(sq_ready.sem, sq_ready.at(l, n0 + j + 1))
                        for tb in range(TB):
                            mm = pe.matmul(bank[7][:, col + tb:col + tb + 1], sq[:, (n0 + j) % 2, tb * P:(tb + 1) * P],
                                           ones[:, 0:1], start=j == 0 and tb == 0, stop=True, skip_group_check=True)
                        mm.then_inc(sq_used.sem, 1)
                elif kind == "cbcast":
                    pe.wait_ge(diag_ready.sem, diag_ready.at(l, 3))
                    for i in range(2):
                        spread(l, 2, diag2[:, i].rearrange("p t n -> p (t n)"), 5 + i, i == 1)
                elif kind == "uq":
                    slot = unit_ready(pe, l, U_OF[it])
                    if it[1] == 0:
                        pe.wait_ge(h_ready.sem, h_ready.at(l, h_at(0) + KD + CN))
                    for i in range(4):
                        if it[1] == 1:
                            pe.wait_ge(qn_evicted.sem, qn_evicted.at(l, i + 1))
                            pe.wait_ge(qr_evicted.sem, qr_evicted.at(l, i + 1))
                        for k in range(2):
                            mm = product(pe, bank[4 + i][:, :], slot, (2 * i + k) * P, slice(0, P), yH[0][:, k],
                                         yL[0][:, k], k == 0, k == 1)
                        mm.then_inc(uq_done.sem if i < 3 else unit_done[slot].sem, 1)
                elif kind == "ukv":
                    slot = unit_ready(pe, l, U_OF[it])
                    for t in range(12):
                        if t < 4:
                            pe.wait_ge(qn_evicted.sem, qn_evicted.at(l, 4 + t + 1))
                            pe.wait_ge(qr_evicted.sem, qr_evicted.at(l, 4 + t + 1))
                        else:
                            pe.wait_ge(kv_evicted.sem, kv_evicted.at(l, t - 3))
                        o = bank[4 + t % 4]
                        if t < HEADS:
                            mm = product(pe, o[:, :], slot, NOPE * t, slice(0, P), yH[0][:, 2], yL[0][:, 2],
                                         True, True)
                        else:
                            tb = slice((t - HEADS) * P, (t - HEADS + 1) * P)
                            vh, vl = wH[:, slot, T:2 * T], wL[:, slot, T:2 * T]
                            pe.matmul(o[:, :], yH[0][:, 2, tb], vh, start=True, stop=False)
                            pe.matmul(o[:, :], yL[0][:, 2, tb], vh, start=False, stop=False)
                            mm = pe.matmul(o[:, :], yH[0][:, 2, tb], vl, start=False, stop=True)
                        mm.then_inc(kv_done.sem if t < 11 else unit_done[slot].sem, 1)
                elif kind == "wi":
                    pe.wait_ge(kv_evicted.sem, kv_evicted.at(l, 12))
                    for tb in range(TB):
                        mm = pe.transpose(bank[6][:, tb * P:(tb + 1) * P], misc[:, tb * P:(tb + 1) * P], ident[:, :])
                    mm.then_inc(wi_psum.sem, 1)
                elif kind == "index":
                    b, h = it[1], it[2]
                    n = HEADS * (b - 1) + h
                    if n >= 2:
                        pe.wait_ge(relu_ready.sem, relu_ready.at(l, n - 1))
                    if n == 0:
                        pe.wait_ge(u_evicted.sem, u_evicted.at(l, U_BANK[("in", "ik", 0)] + 1))
                    rows = slice(64 * (h % 2), 64 * (h % 2) + 64)
                    pe.matmul(bank[4 + n % 2][:, 0:P * (b + 1)], iq[rows, h // 2, b * P:(b + 1) * P],
                              ik[rows, 0:P * (b + 1)], start=True, stop=True).then_inc(dots_ready.sem, 1)
                elif kind == "vtok":
                    br = it[1]
                    src = {"A": av, "D": dv}[br]
                    pe.wait_ge(u_evicted.sem, u_evicted.at(l, U_BANK[("in", {"A": "av", "D": "dv"}[br], 0)] + 1))
                    pe.wait_ge(pt_evicted.sem, pt_evicted.at(l, STEPS * (1 if br == "D" else 2)))
                    for tb in range(TB):
                        mm = pe.transpose(bank[6][:, tb * P:(tb + 1) * P], src[:, tb * P:(tb + 1) * P], ident[:, :])
                    mm.then_inc(vt_psum.sem, 1)
                elif kind == "att":
                    tensor_attention(pe, l, it[1], it[2])
                elif kind == "branch":
                    n, mp = it[1], it[2]
                    slot = U_OF[it] % RING
                    if first:
                        unit_ready(pe, l, U_OF[it])
                    i = Y_OF[n]
                    y_done = V_BANK.get(("y", n, TB - 1), 0) + 1
                    if mp == 0 and n == "B":
                        pe.wait_ge(yb_lo.sem, yb_lo.at(l, LRU_T))
                    for m in range(0 if first else 1, 2 if last else 1):
                        use = V_BANK[("proj", n, 2 * mp + m)]
                        pe.wait_ge(v_evicted.sem, v_evicted.at(l, max(use - 1, y_done)))
                        for k in range(4):
                            mm = product(pe, bank[2 + use % 2][:, :], slot, (4 * m + k) * P, slice(0, P), yH[i][:, k],
                                         yL[i][:, k], k == 0, k == 3)
                    if last:
                        mm.then_inc(unit_done[slot].sem, 1)
                elif kind == "lru":
                    j = it[1]
                    pe.wait_ge(conv_ready.sem, conv_ready.at(l, j + 1))
                    if j == 0:
                        pe.wait_ge(lru_in.sem, lru_in.at(l, 16))
                    else:
                        pe.wait_ge(asq_ready.sem, asq_ready.at(l, j))
                    pe.matmul(bank[4][:, :], lru_w[:, j], xc[:, :], start=True, stop=True)
                    pe.matmul(bank[5][:, :], lru_w[:, LRU_T + j], xc[:, :], start=True, stop=True
                              ).then_inc(lru_psum.sem, 1)
                elif kind == "out":
                    m = it[1]
                    slot = unit_ready(pe, l, U_OF[it])
                    o = bank[4 + m if m < 4 else m - 4]
                    if m == 0:
                        pe.wait_ge(ytok_ready.sem, ytok_ready.at(l, TB * len(ATT)))
                        pe.wait_ge(asq_ready.sem, asq_ready.at(l, LRU_T))
                    if m == 4:
                        pe.wait_ge(v_evicted.sem, v_evicted.at(l, V_USES))
                        pe.wait_ge(u_evicted.sem, u_evicted.at(l, len(U_BANK)))
                    for k in range(KD):
                        if m == 0 and k % 2 == 0:
                            pe.wait_ge(mlo_ready.sem, mlo_ready.at(l, k // 2 + 1))
                        mm = product(pe, o[:, :], slot, k * P, slice(0, P), mH[:, k], mL[:, k], k == 0, k == KD - 1)
                    mm.then_inc(unit_done[slot].sem, 1)
                    if m >= 4:
                        if m == 4:
                            pe.wait_ge(y_saved.sem, y_saved.at(l, 4 + 1))
                        sum_squares(l, sq_at(1, 0) + m - 4, m == 4, False)

        def tensor_attention(pe, l, br, st):
            if st < STEPS:
                g = att_index(br, st)
                b, h, k0, nk = keys(br, st)
                if st == 0:
                    if br == "C":
                        pe.wait_ge(relu_ready.sem, relu_ready.at(l, NI))
                        pe.wait_ge(kr_ready.sem, kr_ready.at(l, 1))
                    elif br == "A":
                        pe.wait_ge(u_evicted.sem, u_evicted.at(l, U_BANK[("in", "ak", 0)] + 1))
                    else:
                        pe.wait_ge(u_evicted.sem, u_evicted.at(l, U_BANK[("in", "dq", 3)] + 1))
                if g >= 2:
                    pe.wait_ge(shifted.sem, shifted.at(l, g - 1))
                q = slice(b * P, (b + 1) * P)
                kk = slice(k0 * P, (k0 + nk) * P)
                if br == "C":
                    a, c = qC[0:96, h, q], kC[0:96, h, kk]
                else:
                    rows = slice(64 * (h // 4), 64 * (h // 4) + 64)
                    qq, kx = (aq, ak) if br == "A" else (dq, dk)
                    a, c = qq[rows, h % 4, q], kx[rows, kk]
                pe.matmul(bank[4 + g % 2][:, 0:P * nk], a, c, start=True, stop=True).then_inc(scores_ready.sem, 1)
            if TR_LAG <= st < STEPS + TR_LAG:
                g = att_index(br, st - TR_LAG)
                b, h, k0, nk = keys(br, st - TR_LAG)
                pe.wait_ge(probs_ready.sem, probs_ready.at(l, g + 1))
                if g >= 1:
                    pe.wait_ge(pt_evicted.sem, pt_evicted.at(l, g))
                if g == STEPS or g == 2 * STEPS:
                    pe.wait_ge(vt_ready.sem, vt_ready.at(l, g // STEPS))
                for i in range(nk):
                    mm = pe.transpose(bank[6][:, i * P:(i + 1) * P], s_sb[:, g % 3, i * P:(i + 1) * P], ident[:, :])
                mm.then_inc(pt_ready.sem, 1)
            if PV_LAG <= st < STEPS + PV_LAG:
                g = att_index(br, st - PV_LAG)
                b, h, k0, nk = keys(br, st - PV_LAG)
                pe.wait_ge(pt_evicted.sem, pt_evicted.at(l, g + 1))
                if h == 0 and g > 0:
                    pe.wait_ge(ytok_ready.sem, ytok_ready.at(l, g // HEADS))
                for i in range(nk):
                    vv = vC[:, k0 + i, h * HD:(h + 1) * HD] if br == "C" else \
                        v_tok[br][:, k0 + i, (h // 4) * HD:(h // 4 + 1) * HD]
                    mm = pe.matmul(bank[7][:, h * HD:(h + 1) * HD], pt_sb[:, g % 2, i * P:(i + 1) * P], vv,
                                   start=i == 0, stop=i == nk - 1)
                mm.then_inc(pv_done.sem, 1)
            blk = (st - YT_LAG) // HEADS
            if st >= YT_LAG and (st - YT_LAG) % HEADS == 0:
                g = TB * ATT.index(br) + blk
                pe.wait_ge(ytok_ready.sem, ytok_ready.at(l, g + 1))
                use = V_BANK[("y", br, blk)]
                pe.wait_ge(v_evicted.sem, v_evicted.at(l, use - 1))
                for t in range(4):
                    mm = pe.transpose(bank[2 + use % 2][:, t * P:(t + 1) * P], y_tok[:, t * P:(t + 1) * P],
                                      ident[:, :])
                mm.then_inc(ytr_ready.sem, 1)

        @block.tensor
        def _(pe):
            def sum_squares(l, n, first, last):
                pe.wait_ge(sq_ready.sem, sq_ready.at(l, n + 1))
                pe.matmul(bank[4][:, :], ones[:, :], sq[:, n % 2], start=first, stop=last).then_inc(sq_used.sem, 1)

            def spread(l, n, src, b, inc=True):
                mm = pe.matmul(bank[b][:, :], ones[:, :], src, start=True, stop=True)
                if inc:
                    mm.then_inc(bc_ready.sem, 1)

            def keep_warm(n, times):
                slot = (U_MIX if n == 0 else U_FFN[1]) % RING
                for _ in range(times):
                    pe.matmul(bank[7][:, :], wH[:, slot, 0:P], wH[:, slot, 0:T], start=True, stop=True)

            def end_of_boundary(l, n):
                for j in range(4, KD):
                    sum_squares(l, sq_at(n, 0) + j, False, j == KD - 1)
                if n < NB - 1:
                    pe.wait_ge(y_saved.sem, y_saved.at(l, 4 * n + 4))
                    unit_ready(pe, l, U_MIX if n == 0 else U_FFN[1])
                    keep_warm(n, WARM[0])
                pe.wait_ge(diag_ready.sem, diag_ready.at(l, norm_at(n, 0) + 1))
                spread(l, n, diag[:, :, :].rearrange("p t n -> p (t n)"), 5)
                if n < NB - 1:
                    keep_warm(n, WARM[1])
                    pre_norm(l, n)

            def pre_norm(l, n):
                for j in range(KD):
                    sum_squares(l, (sq_at(n, 1) if n >= 0 else -KD) + j, j == 0, j == KD - 1)
                    if n >= 0 and j % 2 and j < KD - 1:
                        keep_warm(n, WARM[2])
                if n >= 0:
                    keep_warm(n, WARM[3])
                pe.wait_ge(diag_ready.sem, diag_ready.at(l, (norm_at(n, 1) if n >= 0 else -1) + 1))
                spread(l, n, diag[:, :, :].rearrange("p t n -> p (t n)"), 6)
                if n >= 0:
                    keep_warm(n, WARM[4])

            def ada_sums(b=7):
                for j in range(KD):
                    mm = pe.matmul(bank[b][:, j:j + 1], ada_acc[:, j * P:(j + 1) * P], ones[:, 0:1], start=j == 0,
                                   stop=True, skip_group_check=True)
                mm.then_inc(ada_sum.sem, 1)

            for slot in range(RING):
                pe.sem_inc(unit_done[slot].sem, 1)
            pe.wait_ge(consts_in.sem, 16 * 5)
            pe.sem_inc(sq_used.sem, 2)
            for c in range(2):
                if c > 0:
                    pe.wait_ge(mod_ready.sem, c)
                pe.wait_ge(ada_used.sem, 2 + 8 * (c + 1))
                ada_sums()

            with pe.Fori(0, DEPTH) as l:
                pre_norm(l, -1)
                for f in range(2):
                    u0 = U_FFN[f]

                    c0 = (ADA_OUT + 1) * f

                    def chunk_sums(c):
                        pe.wait_ge(mod_ready.sem, mod_ready.at(l, c))
                        pe.wait_ge(ada_used.sem, ada_used.at(l, 8 * (c + 1)))
                        ada_sums()

                    def turn(i, c=None, units=range(4)):
                        for j in units:
                            if j % 2 == 0:
                                pe.wait_ge(pair_done.sem, pair_done.at(l, f * FT + 2 * i + j // 2 - 1))
                            slot = unit_ready(pe, l, u0 + j, i)
                            for k in range(KD):
                                mm = product(pe, bank[j][:, :], slot, k * P, slice(0, P), hH[:, k], hL[:, k], k == 0,
                                             k == KD - 1)
                            mm.then_inc(unit_done[slot].sem, 1)
                            if c is not None and j == 0:
                                chunk_sums(c)

                    slots = [unit_ready(pe, l, u0 + j) for j in range(LEAD)]
                    pe.wait_ge(pair_done.sem, pair_done.at(l, f * FT))
                    for k in range(KD):
                        pe.wait_ge(h_ready.sem, h_ready.at(l, (h_at(1) if f else -KD) + k + 1))
                        for j, slot in enumerate(slots):
                            mm = product(pe, bank[j][:, :], slot, k * P, slice(0, P), hH[:, k], hL[:, k], k == 0,
                                         k == KD - 1)
                            if k == KD - 1:
                                mm.then_inc(unit_done[slot].sem, 1)
                    turn(0, None, range(LEAD, 4))
                    turn(1)
                    with pe.Fori(1, ADA_FFN[f]) as i:
                        turn(2 * i, i + (c0 - 1))
                        turn(2 * i + 1)
                    chunk_sums(c0 + ADA_FFN[f] - 1)
                    with pe.Fori(2 * ADA_FFN[f], FT // 2) as i:
                        turn(i)
                    n = 2 * f
                    for q in range(FT):
                        a, j = q // (FT // 2), q % (FT // 2)
                        if f == 0 and q == 9:
                            pe.wait_ge(pair_done.sem, pair_done.at(l, FT))
                            pe.wait_ge(mod_ready.sem, mod_ready.at(l, ADA_OUT))
                            pe.wait_ge(ada_used.sem, ada_used.at(l, 8 * (ADA_OUT + 1)))
                            ada_sums(0)
                        if f == 0 and q == FT // 2:
                            pe.wait_ge(mod_ready.sem, mod_ready.at(l, ADA_OUT + 1))
                        slot = unit_ready(pe, l, u0 + 2 * FT + q)
                        for kt in range(2):
                            k = 2 * j + kt
                            if a == 0:
                                pe.wait_ge(ffn_lo.sem, ffn_lo.at(l, f * FT + k + 1))
                            for mt in range(4):
                                mm = product(pe, bank[4 - 4 * a + mt][:, :], slot, kt * T + mt * P, slice(0, P),
                                             fH[:, k], fL[:, k], k == 0, k == FT - 1)
                        mm.then_inc(unit_done[slot].sem, 1)
                        if FT // 2 < q <= FT // 2 + 4:
                            jj = q - FT // 2 - 1
                            if jj == 0:
                                pe.wait_ge(y_saved.sem, y_saved.at(l, 4 * n + 1))
                            sum_squares(l, sq_at(n, 0) + jj, jj == 0, False)
                    end_of_boundary(l, n)
                    if f == 0:
                        tensor_mixer(pe, l, sum_squares, spread)
                        end_of_boundary(l, 1)


def _units(w_ffn_in, w_ffn_out):
    gu = w_ffn_in.reshape(KD, P, 2, FT, P).transpose(3, 2, 1, 0, 4).reshape(2 * FT, P, KD * P)
    wo = w_ffn_out.reshape(FT // 2, 2, P, 2, D // 2).transpose(3, 0, 2, 1, 4).reshape(FT, P, KD * P)
    return [gu, wo]


def _tile(w, cols):
    return w[:, cols].reshape(-1, P, len(cols)).transpose(1, 0, 2).reshape(1, P, -1)


def _mixer_units(w_in, w_uq, w_ukv, w_branch, w_out):
    splits = {}
    at = 0
    for name, n in (("a_q", 512), ("a_k", 128), ("a_v", 128), ("i_q", 512), ("i_k", 64), ("i_w", 8), ("r_x", 512),
                    ("r_g", 512), ("c_q", 256), ("c_kv", 160), ("d_q", 512), ("d_k", 128), ("d_v", 128),
                    ("gates", 4096)):
        splits[name] = at
        at += n
    r = np.arange
    swapped = np.r_[ROPE // 2:ROPE, 0:ROPE // 2]
    pairs = lambda o, j: np.r_[o + 64 * j + r(64), o + 64 * (j + 4) + r(64)]

    def cols(name, j):
        s = splits
        if name == "misc":
            kr = s["c_kv"] + P
            return np.r_[np.tile(s["i_w"] + r(8), 8), kr + r(ROPE), kr + swapped]
        if name == "ik":
            return np.tile(s["i_k"] + r(64), 2)
        if name in ("aq", "dq"):
            return pairs(s[name[0] + "_q"], j)
        o = s[{"cq": "c_q", "ckv": "c_kv", "iq": "i_q", "ak": "a_k", "av": "a_v", "dk": "d_k", "dv": "d_v",
               "rx": "r_x", "rg": "r_g"}[name]]
        return o + P * j + r(P)

    branch_at = {n: i for i, n in enumerate("ABCD")}
    out = []
    for it in MIX_UNITS:
        if it[0] == "in":
            out.append(_tile(w_in, cols(it[1], it[2])))
        elif it[0] == "gate":
            out.append(_tile(w_in, splits["gates"] + branch_at[it[1]] * D + P * it[2] + r(P)))
        elif it[0] == "out":
            out.append(_tile(w_out, P * it[1] + r(P)))
        elif it[0] == "branch":
            w = w_branch[branch_at[it[1]]]
            out.append(np.concatenate([_tile(w, P * (2 * it[2] + m) + r(P)) for m in range(2)], axis=2))
        elif it[0] == "uq":
            heads = [96 * (4 * it[1] + i) for i in range(4)]
            out.append(np.concatenate([_tile(w_uq, np.r_[h + r(96), h + 64 + swapped]) for h in heads], axis=2))
        else:
            out.append(_tile(w_ukv, np.r_[np.concatenate([P * h + r(64) for h in range(HEADS)]),
                                          np.concatenate([P * h + 64 + r(64) for h in range(HEADS)])]))
    return out


def _feature_major(a):
    return np.ascontiguousarray(a).reshape(-1, P).T


def _constants():
    q = np.arange(P)[:, None]
    rel = np.arange(T)[None, :] - (T - P)
    dist = (q - rel).astype(np.float32)
    causal = np.where(rel > q, BIG, 0).astype(np.float32)
    rw = np.arange(2 * P)[None, :] - P
    window = np.where((rw <= q) & (q - rw < P), 0, BIG).astype(np.float32)
    half = ROPE // 2
    inv = (np.float32(10000.0) ** (-np.arange(half, dtype=np.float32) / half)).astype(np.float32)
    ang = np.arange(T, dtype=np.float32)[None, :] * inv[:, None]
    cos, sin = np.cos(ang), np.sin(ang)
    rope = np.zeros((P, T), np.float32)
    rope[64:96] = np.concatenate([cos, cos])
    rope[96:128] = np.concatenate([-sin, sin])
    mixc = np.concatenate([dist, causal, (rope * np.float32(-C_SCALE)).astype(np.float32), rope, window], axis=1)
    return np.concatenate([np.eye(P), np.ones((P, P))], axis=1).astype(np.float32), mixc.astype(np.float32)


def kernel(**inputs):
    import concourse.bacc as bacc
    from concourse.bass_utils import run_bass_kernel_spmd

    a = {k: np.asarray(v) for k, v in inputs.items()}
    parts = []
    for l in range(DEPTH):
        parts += _units(a["ffn1_w_in"][l], a["ffn1_w_out"][l])
        parts += _mixer_units(a["w_in"][l], a["mla_w_uq"][l], a["mla_w_ukv"][l], a["w_branch"][l], a["w_out"][l])
        parts += _units(a["ffn2_w_in"][l], a["ffn2_w_out"][l])
    stream = np.concatenate(parts + [parts[0][:RING]], axis=0)

    w_ada = a["w_ada"].reshape(DEPTH, KD, P, NADA, D).transpose(0, 3, 1, 2, 4)
    nxt = [min(l + 1, DEPTH - 1) for l in range(DEPTH)]
    ada = np.concatenate([np.concatenate([w_ada[l, 2:], w_ada[nxt[l], :2]]) for l in range(DEPTH)])
    ada0 = w_ada[0, :2].reshape(2 * KD, P, D).transpose(1, 0, 2)
    pars = []
    for l in range(DEPTH):
        b, bn = _feature_major(a["b_ada"][l]), _feature_major(a["b_ada"][nxt[l]])
        g, gn = _feature_major(a["norm_g"][l]), _feature_major(a["norm_g"][nxt[l]])
        conv = a["conv_w"][l].reshape(4, LRU_T, P).transpose(2, 1, 0).reshape(P, -1)
        pars.append(np.concatenate(
            [b[:, 2 * KD:], bn[:, :2 * KD], gn[:, :KD], g[:, KD:], conv, _feature_major(a["conv_b"][l]),
             _feature_major(a["lru_ba"][l]), _feature_major(a["lru_bx"][l]), _feature_major(a["lru_lambda"][l]),
             _feature_major(a["mla_g_q"][l]), _feature_major(a["mla_g_kv"][l]),
             np.broadcast_to(a["swa_sinks"][l], (P, HEADS))], axis=1))
    pars = np.stack(pars, axis=1)
    par0 = np.concatenate([_feature_major(a["b_ada"][0])[:, :2 * KD], _feature_major(a["norm_g"][0])[:, :KD]], axis=1)
    lruw = np.zeros((DEPTH, P, 2 * LRU_T, P), np.float32)
    for i, name in enumerate(("lru_wa", "lru_wx")):
        for n in range(8):
            rows = slice(64 * (n % 2), 64 * (n % 2) + 64)
            lruw[:, rows, LRU_T * i + n // 2, rows] = a[name][:, n]
    consts, mixc = _constants()
    arrays = {
        "stream": stream, "ada": ada, "ada0": ada0, "pars": pars, "par0": par0, "cvec": _feature_major(a["c"][0]),
        "consts": consts, "mixc": mixc, "lruw": lruw,
        "x_in": a["x"][0].T.reshape(KD, P, T).transpose(1, 0, 2),
    }
    arrays = {k: np.ascontiguousarray(v) for k, v in arrays.items()}
    nc = bacc.Bacc("TRN2", target_bir_lowering=False, num_devices=1)
    args = [nc.dram_tensor(k, v.shape, F32, kind="ExternalInput").ap() for k, v in arrays.items()]
    args.append(nc.dram_tensor("out", (P, KD, T), F32, kind="ExternalOutput").ap())
    trunk_kernel(nc, *args)
    r = run_bass_kernel_spmd(nc, [arrays], core_ids=[0])
    y = r.results[0]["out"]
    return np.ascontiguousarray(y.transpose(1, 0, 2).reshape(D, T).T)[None]
```
